# Optimizing a Trainium2 kernel written in Bass

```python
import math
import jax, jax.numpy as jnp
from jax import lax
import numpy as np

D_MODEL = 1024
BATCH = 1
SEQ = 512
DEPTH = 2

N_MIXERS = 2
N_POOL_LAYERS = (DEPTH + 1) // 2
N_SSM_LAYERS = DEPTH // 2
RMS_EPS = 1e-5

POOL_WINDOWS = (2, 4, 8, 16)
N_POOL_GROUPS = len(POOL_WINDOWS)
POOL_GROUP = D_MODEL // N_POOL_GROUPS

SSM_EXPAND = 2
D_INNER = SSM_EXPAND * D_MODEL
HEAD_DIM = 64
N_HEADS = D_INNER // HEAD_DIM
N_GROUPS = 4
HEADS_PER_GROUP = N_HEADS // N_GROUPS
D_STATE = 128
CONV_K = 4
CHUNK = 128
CONV_DIM = D_INNER + 2 * N_GROUPS * D_STATE
IN_PROJ_DIM = D_INNER + CONV_DIM + N_HEADS

D_FF = 4 * D_MODEL

kernel_name = "pool_ssd_interleaved_hybrid"

def rms_norm(x, g):
    xf = x.astype(jnp.float32)
    y = xf * lax.rsqrt(jnp.mean(xf * xf, axis=-1, keepdims=True) + RMS_EPS)
    return (y * g.astype(jnp.float32)).astype(x.dtype)

def pool_mixer(h, w_pool, b_pool, scale):
    b, s, d = h.shape
    hf = h.astype(jnp.float32)
    cs = jnp.pad(jnp.cumsum(hf, axis=1), ((0, 0), (1, 0), (0, 0)))
    t = jnp.arange(s)
    hg = hf.reshape(b, s, N_POOL_GROUPS, POOL_GROUP)
    csg = cs.reshape(b, s + 1, N_POOL_GROUPS, POOL_GROUP)
    pooled = []
    for gi, w in enumerate(POOL_WINDOWS):
        c = csg[:, :, gi]
        lower = c[:, jnp.maximum(t + 1 - w, 0)]
        count = jnp.minimum(t + 1, w).astype(jnp.float32)
        pooled.append((c[:, 1:] - lower) / count[None, :, None])
    mixed = jnp.stack(pooled, axis=2) - hg
    out = jnp.einsum("bsgi,gio->bsgo", mixed, w_pool.astype(jnp.float32)).reshape(b, s, d)
    out = (out + b_pool.astype(jnp.float32)) * scale.astype(jnp.float32)
    return out.astype(h.dtype)

def causal_dwconv(u, w, bias):
    s = u.shape[1]
    up = jnp.pad(u, ((0, 0), (CONV_K - 1, 0), (0, 0)))
    out = up[:, 0:s] * w[0]
    for k in range(1, CONV_K):
        out = out + up[:, k:k + s] * w[k]
    return out + bias

def ssd_scan(xs, dt, a, bm, cm):
    b, s, g, r, p = xs.shape
    n = bm.shape[-1]
    nc = s // CHUNK
    x = xs.astype(jnp.float32).reshape(b, nc, CHUNK, g, r, p)
    dtc = dt.astype(jnp.float32).reshape(b, nc, CHUNK, g, r)
    bc = bm.astype(jnp.float32).reshape(b, nc, CHUNK, g, n)
    cc = cm.astype(jnp.float32).reshape(b, nc, CHUNK, g, n)
    xdt = x * dtc[..., None]
    adt = jnp.moveaxis(dtc * a.astype(jnp.float32), 2, -1)
    a_cs = jnp.cumsum(adt, axis=-1)
    causal = jnp.tril(jnp.ones((CHUNK, CHUNK), dtype=bool))
    seg = a_cs[..., :, None] - a_cs[..., None, :]
    decay = jnp.exp(jnp.where(causal, seg, -jnp.inf))
    cb = jnp.einsum("bclgn,bcsgn->bcgls", cc, bc)
    y_diag = jnp.einsum("bcgls,bcgrls,bcsgrp->bclgrp", cb, decay, xdt)
    decay_to_end = jnp.exp(a_cs[..., -1:] - a_cs)
    states = jnp.einsum("bclgn,bcgrl,bclgrp->bcgrpn", bc, decay_to_end, xdt)
    chunk_decay = jnp.exp(a_cs[..., -1])

    def step(hstate, inp):
        st, dec = inp
        return hstate * dec[..., None, None] + st, hstate

    h0 = jnp.zeros((b, g, r, p, n), jnp.float32)
    _, prev = lax.scan(step, h0, (jnp.moveaxis(states, 1, 0), jnp.moveaxis(chunk_decay, 1, 0)))
    prev = jnp.moveaxis(prev, 0, 1)
    y_off = jnp.einsum("bclgn,bcgrpn,bcgrl->bclgrp", cc, prev, jnp.exp(a_cs))
    return (y_diag + y_off).reshape(b, s, g, r, p)

def ssd_mixer(h, w_in, conv_w, conv_b, dt_bias, a_log, d_skip, norm_g, w_out):
    b, s, _ = h.shape
    zxbcdt = h @ w_in
    z = zxbcdt[..., :D_INNER]
    xbc = zxbcdt[..., D_INNER:D_INNER + CONV_DIM]
    dt_raw = zxbcdt[..., D_INNER + CONV_DIM:]
    xbc = jax.nn.silu(causal_dwconv(xbc, conv_w, conv_b))
    xs = xbc[..., :D_INNER].reshape(b, s, N_GROUPS, HEADS_PER_GROUP, HEAD_DIM)
    bm = xbc[..., D_INNER:D_INNER + N_GROUPS * D_STATE].reshape(b, s, N_GROUPS, D_STATE)
    cm = xbc[..., D_INNER + N_GROUPS * D_STATE:].reshape(b, s, N_GROUPS, D_STATE)
    dt = jax.nn.softplus(dt_raw.astype(jnp.float32) + dt_bias.astype(jnp.float32))
    dt = dt.reshape(b, s, N_GROUPS, HEADS_PER_GROUP)
    a = -jnp.exp(a_log.astype(jnp.float32)).reshape(N_GROUPS, HEADS_PER_GROUP)
    y = ssd_scan(xs, dt, a, bm, cm)
    y = y + d_skip.astype(jnp.float32).reshape(N_GROUPS, HEADS_PER_GROUP)[..., None] * xs.astype(jnp.float32)
    y = y.reshape(b, s, D_INNER) * jax.nn.silu(z.astype(jnp.float32))
    yg = y.reshape(b, s, N_GROUPS, D_INNER // N_GROUPS)
    yg = yg * lax.rsqrt(jnp.mean(yg * yg, axis=-1, keepdims=True) + RMS_EPS)
    y = (yg.reshape(b, s, D_INNER) * norm_g.astype(jnp.float32)).astype(h.dtype)
    return y @ w_out

def sq_relu_mlp(h, w1, w2):
    u = jax.nn.relu(h @ w1)
    return (u * u) @ w2

def setup_inputs(seed: int = 0) -> dict:
    key = jax.random.key(seed)
    ks = jax.random.split(key, 20)
    f32 = jnp.float32
    nrm = lambda k, shape, scale: jax.random.normal(k, shape, f32) * scale
    x = jax.random.normal(ks[0], (BATCH, SEQ, D_MODEL), f32)
    norm_mix_g = 1.0 + nrm(ks[1], (DEPTH, D_MODEL), 0.05)
    norm_mlp_g = 1.0 + nrm(ks[2], (DEPTH, D_MODEL), 0.05)
    pool_w = nrm(ks[3], (N_POOL_LAYERS, N_POOL_GROUPS, POOL_GROUP, POOL_GROUP), POOL_GROUP ** -0.5)
    pool_b = nrm(ks[4], (N_POOL_LAYERS, D_MODEL), 0.02)
    pool_scale = 0.5 + nrm(ks[5], (N_POOL_LAYERS, D_MODEL), 0.05)
    ssm_w_in = nrm(ks[6], (N_SSM_LAYERS, D_MODEL, IN_PROJ_DIM), D_MODEL ** -0.5)
    ssm_conv_w = nrm(ks[7], (N_SSM_LAYERS, CONV_K, CONV_DIM), CONV_K ** -0.5)
    ssm_conv_b = nrm(ks[8], (N_SSM_LAYERS, CONV_DIM), 0.02)
    dt0 = jnp.exp(jax.random.uniform(ks[9], (N_SSM_LAYERS, N_HEADS), f32)
                  * (math.log(0.1) - math.log(0.001)) + math.log(0.001))
    ssm_dt_bias = dt0 + jnp.log(-jnp.expm1(-dt0))
    ssm_a_log = jnp.log(jax.random.uniform(ks[10], (N_SSM_LAYERS, N_HEADS), f32, 1.0, 16.0))
    ssm_d = 1.0 + nrm(ks[11], (N_SSM_LAYERS, N_HEADS), 0.1)
    ssm_norm_g = 1.0 + nrm(ks[12], (N_SSM_LAYERS, D_INNER), 0.05)
    ssm_w_out = nrm(ks[13], (N_SSM_LAYERS, D_INNER, D_MODEL), D_INNER ** -0.5)
    mlp_w1 = nrm(ks[14], (DEPTH, D_MODEL, D_FF), D_MODEL ** -0.5)
    mlp_w2 = nrm(ks[15], (DEPTH, D_FF, D_MODEL), D_FF ** -0.5)
    final_g = 1.0 + nrm(ks[16], (D_MODEL,), 0.05)
    return {"x": x, "norm_mix_g": norm_mix_g, "norm_mlp_g": norm_mlp_g,
            "pool_w": pool_w, "pool_b": pool_b, "pool_scale": pool_scale,
            "ssm_w_in": ssm_w_in, "ssm_conv_w": ssm_conv_w, "ssm_conv_b": ssm_conv_b,
            "ssm_dt_bias": ssm_dt_bias, "ssm_a_log": ssm_a_log, "ssm_d": ssm_d,
            "ssm_norm_g": ssm_norm_g, "ssm_w_out": ssm_w_out,
            "mlp_w1": mlp_w1, "mlp_w2": mlp_w2, "final_g": final_g}

def reference(x, norm_mix_g, norm_mlp_g, pool_w, pool_b, pool_scale,
              ssm_w_in, ssm_conv_w, ssm_conv_b, ssm_dt_bias, ssm_a_log, ssm_d,
              ssm_norm_g, ssm_w_out, mlp_w1, mlp_w2, final_g):
    h = x
    for i in range(DEPTH):
        hn = rms_norm(h, norm_mix_g[i])
        if i % N_MIXERS == 0:
            j = i // N_MIXERS
            mix = pool_mixer(hn, pool_w[j], pool_b[j], pool_scale[j])
        else:
            j = i // N_MIXERS
            mix = ssd_mixer(hn, ssm_w_in[j], ssm_conv_w[j], ssm_conv_b[j], ssm_dt_bias[j],
                            ssm_a_log[j], ssm_d[j], ssm_norm_g[j], ssm_w_out[j])
        h = h + mix
        h = h + sq_relu_mlp(rms_norm(h, norm_mlp_g[i]), mlp_w1[i], mlp_w2[i])
    return rms_norm(h, final_g)


_drawn_inputs = setup_inputs


def setup_inputs(seed=0):
    import zlib

    import numpy as np

    out = dict(_drawn_inputs(seed))
    spreads = {}
    factors = {'pool_b': 4.522, 'ssm_conv_b': 3.929}
    for name, (base, spread) in spreads.items():
        noise = np.random.default_rng([zlib.crc32(name.encode()), seed]).standard_normal(out[name].shape)
        drawn = base * np.exp(spread * noise) if base else spread * noise
        out[name] = __import__('jax').numpy.asarray(drawn.astype(out[name].dtype))
    for name, factor in factors.items():
        out[name] = (out[name] * factor).astype(out[name].dtype)
    return out
```

```python
from contextlib import ExitStack

import concourse.bass as bass
from concourse import mybir
from concourse.alu_op_type import AluOpType as ALU

F32 = mybir.dt.float32
F32R = mybir.dt.float32r
ACT = mybir.ActivationFunctionType

P = 128
TOK = 512
D_MODEL = 1024
KD = D_MODEL // P
D_FF = 4096
WINDOWS = (2, 4, 8, 16)
PAD = 16
HEADS, HD, GROUPS, CHUNKS, CONV_K = 32, 64, 4, 4, 4
HPG = HEADS // GROUPS
GT = HPG * HD // P
D_INNER = HEADS * HD
CONVS = GT + 2
EPS = 1e-5
N_SOFT = 7

U_POOL = 0
U_MLP0 = 2
BLK = 16
U_SSM = U_MLP0 + 64
U_GROUP = U_SSM + 7
PER_GROUP = GT + CONVS
U_OUT = U_SSM + 1 + 4 * PER_GROUP
U_MLP1 = U_OUT + 16
UNITS = U_MLP1 + 64
A_MLP0 = 8
A_SSM = A_MLP0 + 48
A_OUT = A_SSM + 1 + 4 * PER_GROUP
A_MLP1 = A_OUT + 16
COLS = {}
_at = 0
for _name, _n in (("g0", 8), ("g1", 8), ("g2", 8), ("g3", 8), ("gf", 8), ("pool_b", 8),
                  ("pool_scale", 8), ("conv_w", 96), ("conv_b", 24), ("norm_g", 16), ("skip", 16),
                  ("dt_bias", 32), ("a_log", 32)):
    COLS[_name] = _at
    _at += _n
N_PARAMS = _at
CHUNK_AFTER = {3: 0, 4: 1, 6: 2, 7: 3}


def build(nc, xt, weights, params, consts, out_t):
    ctx = ExitStack()
    with ctx:
        sem = lambda name: ctx.enter_context(nc.semaphore(name))
        at = [nc.sbuf_base + 63 & ~63]

        def sb(name, shape, dtype=F32, offset=None):
            size = 4
            for n in shape[1:]:
                size *= n
            where = at[0] if offset is None else offset
            if offset is None:
                at[0] += size + 31 & ~31
            t = nc.alloc_sbuf_tensor_at(name, shape, dtype, offset=where)
            return t, where

        h, _ = sb("residual", [P, KD, TOK])
        xhi, _ = sb("x_hi", [P, KD, TOK], F32R)
        xhi_f = xhi[:, :, :].bitcast(F32)
        xlo, o_xlo = sb("x_lo", [P, KD, TOK], F32R)
        hg, _ = sb("scaled_residual", [P, KD, TOK], F32, o_xlo)
        act_hi, o_hi = sb("act_hi", [P, BLK, TOK], F32R)
        act_hi_f = act_hi[:, :, :].bitcast(F32)
        act_lo, o_lo = sb("act_lo", [P, BLK, TOK], F32R)
        yx, _ = sb("y_accumulated", [P, BLK, TOK], F32, o_lo)
        zs, _ = sb("z_silu", [P, BLK, TOK], F32, o_hi)
        xact, _ = sb("x_conv", [P, GT, TOK], F32, o_hi + 12 * TOK * 4)
        padded = [sb(f"padded{i}", [P, PAD + TOK], F32, o_hi + i * 2176)[0] for i in range(3)]
        mixed, _ = sb("mixed", [P, TOK], F32, o_hi + 3 * 2176)
        raw, _ = sb("w_raw", [P, 2, 1024])
        whi, _ = sb("w_hi", [P, 2, 1024], F32R)
        whi_f = whi[:, :, :].bitcast(F32)
        wlo, _ = sb("w_lo", [P, 2, 1024], F32R)
        prm, _ = sb("params", [P, N_PARAMS])
        cst, _ = sb("constants", [P, 3 * P + 4 * PAD])
        ones, upper, ident = (cst[:, i * P:(i + 1) * P] for i in range(3))
        inv_count = cst[:, 3 * P:].rearrange("p (g c) -> p g c", g=4)
        tmp, _ = sb("tmp", [P, 2, TOK])
        sq, o_sq = sb("squares", [P, GT, TOK])
        ssq, _ = sb("square_sum", [P, TOK])
        rstd, _ = sb("rstd", [P, TOK])
        pre, _ = sb("conv_in", [P, CONV_K - 1 + TOK])
        bf, _ = sb("b_feature", [P, TOK])
        cf, _ = sb("c_feature", [P, GROUPS, TOK])
        xdt, _ = sb("x_dt", [P, CHUNKS, TOK])
        bt, _ = sb("b_token", [P, CHUNKS, P])
        cbm, _ = sb("cb_masked", [P, CHUNKS, P])
        dec, _ = sb("x_dt_decayed", [P, 2, TOK])
        mbuf, _ = sb("m", [P, 2, HPG * P])
        e2, _ = sb("decay_in", [P, 2, GT, P])
        state, _ = sb("state", [P, TOK])
        ytmp, _ = sb("y_tmp", [P, TOK])
        rg, _ = sb("group_rstd", [P, TOK])
        hd4 = [P, CHUNKS, HEADS]
        dtx, _ = sb("dt_x", hd4)
        neg_abs, _ = sb("dt_neg_abs", hd4)
        ex, _ = sb("dt_exp", hd4)
        mx, _ = sb("dt_max", hd4)
        rc, _ = sb("dt_rc", hd4)
        ser, _ = sb("dt_series", hd4)
        s2, _ = sb("dt_s2", hd4)
        dt_t, _ = sb("dt_token", hd4)
        adt, _ = sb("a_dt", hd4)
        exp_a, _ = sb("exp_a", [P, HEADS])
        cum, _ = sb("cumulated", [P, 2, CHUNKS * HEADS])
        acs_t = cum[:, 0, :]
        dend, _ = sb("decay_to_end", [P, CHUNKS * HEADS])
        cd, _ = sb("chunk_decay", [P, CHUNKS * HEADS])
        acs_f, _ = sb("a_cs_feature", [HEADS, TOK], F32, o_sq)
        eacs_f, _ = sb("exp_a_cs_feature", [HEADS, TOK], F32, o_sq + TOK * 4)
        assert at[0] <= nc.sbuf_usable_end, (at[0], nc.sbuf_usable_end)

        acs_dram = nc.dram_tensor("acs_scratch", [GROUPS, CHUNKS, HPG, P], F32).ap()
        eacs_dram = nc.dram_tensor("eacs_scratch", [GROUPS, CHUNKS, HPG, P], F32).ap()

        bank = [ctx.enter_context(nc.psum_tensor(f"bank{i}", [P, TOK], F32)) for i in range(8)]
        acc = bank[0:2]
        pool_acc = bank
        XT_BANK = (bank[2], bank[4], bank[5], bank[6])
        b_misc, b_yd, b_yo, b_st, b_stat = bank[3], bank[4], bank[5], bank[6], bank[7]

        x_landed = [sem(f"x_landed{m}") for m in range(KD)]
        params_landed = sem("params_landed")
        consts_landed = sem("consts_landed")
        raw_landed = [sem("raw_landed0"), sem("raw_landed1")]
        hi_ready = sem("w_hi_ready")
        lo_ready = sem("w_lo_ready")
        wt_used = sem("w_used")
        acc_drained = sem("acc_drained")
        h_done = sem("h_done")
        xhi_ready = sem("x_hi_ready")
        xlo_ready = sem("x_lo_ready")
        sq_ready = sem("sq_ready")
        ssq_clear = sem("ssq_clear")
        ssq_added = sem("ssq_added")
        stat_ready = sem("stat_ready")
        stat_drained = sem("stat_drained")
        sqrt_done = sem("sqrt_done")
        recip_done = sem("recip_done")
        pads_clear = sem("pads_clear")
        chain = sem("dve_chain")
        hid_sq_ready = sem("hidden_square_ready")
        hid_hi_ready = sem("hidden_hi_ready")
        hid_lo_ready = sem("hidden_lo_ready")
        conv_step = sem("conv_step")
        conv_ready = sem("conv_ready")
        silu_done = sem("silu_done")
        skip_ready = sem("skip_ready")
        dtt_ready = sem("dt_transposed")
        dt_na = sem("dt_neg_abs_ready")
        dt_exp = sem("dt_exp_ready")
        adt_ready = sem("adt_ready")
        cum_ready = sem("cum_ready")
        acsf_ready = sem("acs_f_ready")
        dend_in = sem("decay_exponent_ready")
        decays = sem("decays_ready")
        scratch = sem("scratch_written")
        tok_ready = sem("token_major_ready")
        xdt_ready = sem("x_dt_ready")
        cbm_ready = sem("cb_ready")
        bt_ready = sem("b_token_ready")
        dec_ready = sem("dec_ready")
        m_landed = [sem("m_landed0"), sem("m_landed1")]
        e_landed = [sem("e_landed0"), sem("e_landed1")]
        seg_step = sem("segment_step")
        seg_ready = sem("segment_ready")
        exp_done = sem("exp_done")
        m_ready = sem("m_ready")
        yd_ready = sem("y_diag_ready")
        yo_ready = sem("y_off_ready")
        st_ready = sem("state_ready")
        y_step = sem("y_step")
        y_done = sem("y_done")
        h_step = sem("state_step")
        state_ready = sem("state_updated")
        gated = sem("gated")
        yn_ready = sem("y_normed")
        yhi_ready = sem("y_hi_ready")
        ylo_ready = sem("y_lo_ready")
        hg_ready = sem("scaled_ready")
        out_ready = sem("out_ready")
        out_ready_pool = sem("out_ready_pool")
        out_written = sem("out_written")

        def col(name, i, n=1):
            return prm[:, bass.ds(COLS[name] + i, n)]

        prep_from = [None, (h_done, 0), (h_done, 16), (acc_drained, A_OUT + 8), (h_done, 32)]
        gains = ["g0", "g1", "g2", "g3", "gf"]
        sq_base = [0, 8, 16, 40, 48]
        add_base = [0, 8, 16, 36, 44]
        stat_of = [0, 1, 2, 7, 8]

        block = ctx.enter_context(nc.Block())

        @block.sync
        def _(sp):
            def load_weights(c, r=0):
                if c >= 2:
                    sp.wait_ge(lo_ready, 2 * (c - 1) + 2 * r)
                sp.dma_start(raw[:, c % 2, :], weights[bass.ds(c + r, 1), :, :].rearrange("a p n -> (a p) n")
                             ).then_inc(raw_landed[c % 2], 16)

            def load_acs(g, c):
                sp.dma_start(mbuf[:, c % 2, :],
                             acs_dram[bass.ds(g, 1), c, :, :].rearrange("g h t -> g (h t)")
                             .to_broadcast([P, HPG * P])).then_inc(m_landed[c % 2], 16)

            def load_exp_acs(g, c):
                heads = eacs_dram[bass.ds(g, 1), c, :, :].rearrange("g (i two) t -> g two i t", two=2)
                for half in range(2):
                    sp.dma_start(e2[64 * half:64 * half + 64, c % 2, :, :],
                                 heads[:, half, :, :].to_broadcast([64, GT, P])).then_inc(e_landed[c % 2], 16)

            for m in range(KD):
                sp.dma_start(h[:, m, :], xt[m, :, :]).then_inc(x_landed[m], 16)
            load_weights(0)
            load_weights(1)
            with sp.Fori(0, (U_GROUP - 1) // 2 - 1) as i:
                load_weights(2, 2 * i)
                load_weights(3, 2 * i)
            load_weights(U_GROUP - 1)
            load_weights(U_GROUP)
            sp.wait_ge(acsf_ready, 1)
            sp.wait_ge(decays, 3)
            for g in range(GROUPS):
                for src, dst in ((acs_f, acs_dram), (eacs_f, eacs_dram)):
                    sp.dma_start(dst[g].rearrange("c h t -> h c t"),
                                 src[g * HPG:(g + 1) * HPG, :].rearrange("h (c t) -> h c t", c=CHUNKS)
                                 ).then_inc(scratch, 16)
            load_weights(U_GROUP + 1)
            load_weights(U_GROUP + 2)
            sp.wait_ge(scratch, 2 * GROUPS * 16)
            load_acs(0, 0)
            load_acs(0, 1)
            load_exp_acs(0, 1)
            load_exp_acs(0, 2)

            def group_loads(g, r, nxt):
                for t in range(PER_GROUP):
                    load_weights(U_GROUP + 3 + t, r)
                    if t == 4:
                        sp.wait_ge(yd_ready, 4 * g + 1)
                        load_acs(g, 2)
                    if t == 5:
                        sp.wait_ge(yd_ready, 4 * g + 2)
                        load_acs(g, 3)
                    if t == 6:
                        sp.wait_ge(y_done, 4 * g + 2)
                        load_exp_acs(g, 3)
                    if nxt and t == 7:
                        sp.wait_ge(yd_ready, 4 * g + 3)
                        load_acs(g + 1, 0)
                    if nxt and t == 8:
                        sp.wait_ge(yd_ready, 4 * g + 4)
                        load_acs(g + 1, 1)
                        sp.wait_ge(y_done, 4 * g + 3)
                        load_exp_acs(g + 1, 2)
                    if nxt and t == 9:
                        sp.wait_ge(y_done, 4 * g + 4)
                        load_exp_acs(g + 1, 1)

            with sp.Fori(0, GROUPS - 1) as g:
                group_loads(g, PER_GROUP * g, True)
            group_loads(GROUPS - 1, PER_GROUP * (GROUPS - 1), False)
            first = U_GROUP + 3 + 4 * PER_GROUP
            with sp.Fori(0, (UNITS - first) // 2) as i:
                load_weights(first, 2 * i)
                load_weights(first + 1, 2 * i)
            for u in range(first + (UNITS - first) // 2 * 2, UNITS):
                load_weights(u)
            for m in range(KD):
                if m % 3 == 2:
                    sp.wait_ge(out_ready_pool, m // 3 + 1)
                else:
                    sp.wait_ge(out_ready, m - (m + 1) // 3 + 1)
                sp.dma_start(out_t[m, :, :], hg[:, m, :]).then_inc(out_written, 16)
            sp.wait_ge(out_written, 16 * KD)

        @block.scalar
        def _(act):
            act.dma_start(prm[:, :], params).then_inc(params_landed, 16)
            act.dma_start(cst[:, :], consts).then_inc(consts_landed, 16)

            def round_weights(c, r=0):
                if c + (r if isinstance(r, int) else 0) >= UNITS:
                    return
                act.wait_ge(raw_landed[c % 2], 16 * (c // 2 + 1) + 8 * r)
                for half in range(2):
                    if c >= 2:
                        act.wait_ge(wt_used, 2 * (c - 2) + half + 1 + 2 * r)
                    part = slice(512 * half, 512 * half + 512)
                    act.activation(whi[:, c % 2, part], raw[:, c % 2, part], ACT.Copy).then_inc(hi_ready, 1)

            def square(m, slot):
                act.activation(sq[:, slot, :], h[:, bass.ds(m, 1), :].rearrange("p a t -> p (a t)"),
                               ACT.Square).then_inc(sq_ready, 1)

            def prepare(n, m, slot, last=False):
                if n or m >= 2:
                    act.wait_ge(ssq_added, add_base[n] + m - 1)
                if n == 0:
                    act.wait_ge(x_landed[m], 16)
                else:
                    s, count = prep_from[n]
                    act.wait_ge(s, count + m + 1)
                if last:
                    act.activation(hg[:, bass.ds(m, 1), :], h[:, bass.ds(m, 1), :], ACT.Copy,
                                   scale=col(gains[n], m)).then_inc(hg_ready, 1)
                else:
                    act.activation(xhi[:, bass.ds(m, 1), :], h[:, bass.ds(m, 1), :], ACT.Copy,
                                   scale=col(gains[n], m)).then_inc(xhi_ready, 1)
                square(m, slot)

            def root(k, buf):
                act.wait_ge(stat_drained, k + 1)
                act.activation(buf[:, :], buf[:, :], ACT.Sqrt).then_inc(sqrt_done, 1)

            act.wait_ge(params_landed, 16)
            for m in range(KD):
                prepare(0, m, m % 2)
            round_weights(0)
            round_weights(1)
            root(0, rstd)
            for u in range(2):
                round_weights(u + 2)
            for m in range(KD):
                prepare(1, m, m % 2)

            def mlp(u0, blk_base, n_next):
                for blk in range(2):
                    hid = blk_base + 16 * blk
                    with act.Fori(0, BLK // 2) as i:
                        for e in range(2):
                            round_weights(u0 + 32 * blk + e + 2, 2 * i)
                            act.wait_ge(hid_sq_ready, hid + e + 1 + 2 * i)
                            act.activation(act_hi[:, bass.ds(2 * i + e, 1), :], tmp[:, e:e + 1, :],
                                           ACT.Copy).then_inc(hid_hi_ready, 1)

                    def down(i, r):
                        for e in range(4):
                            round_weights(u0 + 32 * blk + BLK + e + 2, r)
                            if blk == 1 and e % 2:
                                prepare(n_next, 2 * i + e // 2, e // 2, n_next == 4)

                    with act.Fori(0, 3) as i:
                        down(i, 4 * i)
                    down(3, 12)

            mlp(U_MLP0, 0, 2)

            def silu(dst, slot):
                act.activation(dst, tmp[:, slot:slot + 1, :], ACT.Silu).then_inc(silu_done, 1)

            def conv_tile(g, q):
                act.wait_ge(conv_ready, CONVS * g + q + 1)
                dst = (bf[:, :].unsqueeze(1) if q == 0 else cf[:, bass.ds(g, 1), :] if q == 1
                       else xact[:, q - 2:q - 1, :])
                silu(dst, (q + 1) % 2)
                if q >= 2:
                    act.wait_ge(silu_done, PER_GROUP * g + q + 1)
                    act.activation(yx[:, bass.ds(GT * g + q - 2, 1), :], xact[:, q - 2:q - 1, :], ACT.Copy,
                                   scale=col("skip", GT * g + q - 2)).then_inc(skip_ready, 1)

            round_weights(U_SSM + 2)
            root(2, rstd)
            act.activation(exp_a[:, :], col("a_log", 0, HEADS), ACT.Exp).then_inc(dt_exp, 1)
            round_weights(U_SSM + 3)
            conv_tile(0, 0)
            act.wait_ge(dt_na, 1)
            act.activation(ex[:, :, :], neg_abs[:, :, :], ACT.Exp).then_inc(dt_exp, 1)
            for q in range(1, CONVS):
                round_weights(U_SSM + 3 + q)
                conv_tile(0, q)
                if q == 2:
                    act.wait_ge(dend_in, 1)
                    act.activation(dend[:, :], dend[:, :], ACT.Exp).then_inc(decays, 1)
                    act.activation(cd[:, :], cum[:, 1, :], ACT.Exp).then_inc(decays, 1)
                    act.wait_ge(acsf_ready, 1)
                    act.activation(eacs_f[:, :], acs_f[:, :], ACT.Exp).then_inc(decays, 1)

            def exp_segments(g, c):
                act.wait_ge(seg_ready, 4 * g + c + 1)
                act.activation(mbuf[:, c % 2, :], mbuf[:, c % 2, :], ACT.Exp).then_inc(exp_done, 1)

            def group(g, r, last):
                for t in range(PER_GROUP + (2 if last else 0)):
                    round_weights(U_GROUP + t + 2, r)
                    if t in (2, 3, 5, 6):
                        exp_segments(g, {2: 0, 3: 1, 5: 2, 6: 3}[t])
                    if t < GT:
                        act.wait_ge(acc_drained, A_SSM + 8 + t + r)
                        if t == 0:
                            act.wait_ge(tok_ready, 6 * g + CHUNKS)
                        silu(zs[:, bass.ds(GT * g + t, 1), :], (t + 1) % 2)
                    elif not last:
                        conv_tile(g + 1, t - GT)
                    if t == 0:
                        act.wait_ge(tok_ready, 6 * g + CHUNKS + 1)
                        act.activation(bt[:, :, :], b_misc[:, :].rearrange("p (c n) -> p c n", c=CHUNKS),
                                       ACT.Copy).then_inc(bt_ready, 1)
                    if t == 8:
                        act.wait_ge(gated, g + 1)
                        for i in range(GT):
                            act.activation(sq[:, i:i + 1, :], yx[:, bass.ds(GT * g + i, 1), :],
                                           ACT.Square).then_inc(sq_ready, 1)
                    if t == 9:
                        root(3 + g, rg)

            with act.Fori(0, GROUPS - 1) as g:
                group(g, PER_GROUP * g, False)
            group(GROUPS - 1, PER_GROUP * (GROUPS - 1), True)
            for m in range(KD):
                round_weights(U_OUT + 8 + m + 2)
                prepare(3, m, m % 2)

            mlp(U_MLP1, 32, 4)
            root(8, rstd)

        @block.gpsimd
        def _(pool):
            pool.memset(pre[:, 0:CONV_K - 1], 0.0).then_inc(pads_clear, 1)
            for i in range(3):
                pool.memset(padded[i][:, 0:PAD], 0.0).then_inc(pads_clear, 1)

            def split_weights(c, r=0):
                if c + (r if isinstance(r, int) else 0) >= UNITS:
                    return
                for half in range(2):
                    pool.wait_ge(hi_ready, 2 * c + half + 1 + 2 * r)
                    part = slice(512 * half, 512 * half + 512)
                    pool.tensor_tensor(wlo[:, c % 2, part], raw[:, c % 2, part], whi_f[:, c % 2, part],
                                       ALU.subtract).then_inc(lo_ready, 1)

            def clear_sum(n):
                if n > 0:
                    pool.wait_ge(stat_ready, stat_of[n])
                pool.memset(ssq[:, :], 0.0).then_inc(ssq_clear, 1)
                pool.wait_ge(ssq_clear, n + 1)

            def add_squares(n, m, slot):
                pool.wait_ge(sq_ready, sq_base[n] + m + 1)
                if n or m:
                    pool.wait_ge(ssq_added, add_base[n] + m)
                pool.tensor_tensor(ssq[:, :], ssq[:, :], sq[:, slot, :], ALU.add).then_inc(ssq_added, 1)

            clear_sum(0)
            for m in range(KD):
                add_squares(0, m, m % 2)
            for u in range(4):
                split_weights(u)
            clear_sum(1)
            for m in range(KD):
                add_squares(1, m, m % 2)

            def mlp(u0, n_next):
                for blk in range(2):
                    with pool.Fori(0, BLK // 2) as i:
                        for e in range(2):
                            split_weights(u0 + 32 * blk + e + 2, 2 * i)
                    if blk == 1:
                        clear_sum(n_next)

                    def down(i, r):
                        for e in range(4):
                            split_weights(u0 + 32 * blk + BLK + e + 2, r)
                            if blk == 1 and e % 2:
                                add_squares(n_next, 2 * i + e // 2, e // 2)

                    with pool.Fori(0, 3) as i:
                        down(i, 4 * i)
                    down(3, 12)

            mlp(U_MLP0, 2)
            for j in range(7):
                split_weights(U_SSM + 2 + j)

            def decayed(g, c):
                pool.wait_ge(xdt_ready, 4 * g + c + 1)
                if c == 2:
                    pool.wait_ge(st_ready, 3 * g + 1)
                pool.tensor_tensor(
                    dec[:, c % 2, :].rearrange("p (h d) -> p h d", h=HPG),
                    xdt[:, c, :].rearrange("p (h d) -> p h d", h=HPG),
                    dend[:, bass.ds(HEADS * c + HPG * g, HPG)].unsqueeze(2).to_broadcast([P, HPG, HD]),
                    ALU.mult).then_inc(dec_ready, 1)

            def group(g, r, last):
                for t in range(PER_GROUP + (2 if last else 0)):
                    split_weights(U_GROUP + 2 + t, r)
                    if t == 0:
                        pool.wait_ge(decays, 1)
                        decayed(g, 0)
                        decayed(g, 1)
                    if t == 3:
                        decayed(g, 2)
                    if t == 8:
                        pool.wait_ge(stat_ready, 3 + g)
                        for i in range(1, GT):
                            pool.wait_ge(sq_ready, 24 + GT * g + i + 1)
                            if i > 1:
                                pool.wait_ge(ssq_added, 24 + (GT - 1) * g + i - 1)
                            pool.tensor_tensor(ssq[:, :], sq[:, 0, :] if i == 1 else ssq[:, :], sq[:, i, :],
                                               ALU.add).then_inc(ssq_added, 1)
                    if t == 9:
                        for i in range(GT):
                            pool.wait_ge(yhi_ready, GT * g + i + 1)
                            tile = bass.ds(GT * g + i, 1)
                            pool.tensor_tensor(act_lo[:, tile, :], yx[:, tile, :], act_hi_f[:, tile, :],
                                               ALU.subtract).then_inc(ylo_ready, 1)

            with pool.Fori(0, GROUPS - 1) as g:
                group(g, PER_GROUP * g, False)
            group(GROUPS - 1, PER_GROUP * (GROUPS - 1), True)
            clear_sum(3)
            for m in range(KD):
                split_weights(U_OUT + 8 + m + 2)
                add_squares(3, m, m % 2)
            mlp(U_MLP1, 4)
            pool.wait_ge(recip_done, 9)
            for m in range(2, KD, 3):
                pool.wait_ge(hg_ready, m + 1)
                pool.tensor_tensor(hg[:, m, :], hg[:, m, :], rstd[:, :], ALU.mult).then_inc(out_ready_pool, 1)

        @block.tensor
        def _(pe):
            def three(out, wh, wl, xh, xl, start, stop):
                pe.matmul(out, wh, xh, start=start, stop=False)
                pe.matmul(out, wh, xl, start=False, stop=False)
                return pe.matmul(out, wl, xh, start=False, stop=stop)

            def unit(c, r, out, hi, lo, tile0, start=True, stop=True, tile_wait=None):
                for k in range(8):
                    if k % 4 == 0:
                        pe.wait_ge(lo_ready, 2 * c + k // 4 + 1 + 2 * r)
                    if tile_wait is not None:
                        tile_wait(k)
                    w = slice(P * k, P * k + P)
                    last = three(out, whi[:, c % 2, w], wlo[:, c % 2, w], hi[:, tile0 + k, :],
                                 lo[:, tile0 + k, :], start and k == 0, stop and k == 7)
                    if k % 4 == 3:
                        last.then_inc(wt_used, 1)

            def accumulator(a, r=0):
                pe.wait_ge(acc_drained, a - 1 + r)
                return acc[a % 2][:, :]

            def statistic(tiles):
                pe.wait_ge(ssq_added, tiles)
                pe.matmul(b_stat[:, :], ones, ssq[:, :], start=True, stop=True).then_inc(stat_ready, 1)

            pe.wait_ge(consts_landed, 16)
            statistic(8)

            for gi in range(len(WINDOWS)):
                pe.wait_ge(lo_ready, gi + 1)
                pe.wait_ge(xlo_ready, 2 * gi + 2)
                if gi == 3:
                    pe.wait_ge(stat_drained, 1)
                for mt in range(2):
                    for k in range(2):
                        w = bass.ds(512 * (gi % 2) + 256 * mt + 128 * k, P)
                        last = three(pool_acc[2 * gi + mt][:, :], whi[:, gi // 2, w], wlo[:, gi // 2, w],
                                     xhi[:, 2 * gi + k, :], xlo[:, 2 * gi + k, :], k == 0, k == 1)
                last.then_inc(wt_used, 1)

            def mlp(u0, a0, x_base, hid_base, squares):
                for blk in range(2):
                    with pe.Fori(0, BLK // 2) as i:
                        for e in range(2):
                            out = accumulator(a0 + 24 * blk + e, 2 * i)
                            unit(u0 + 32 * blk + e, 2 * i, out, xhi, xlo, 0,
                                 tile_wait=(lambda k: pe.wait_ge(xlo_ready, x_base + k + 1)) if e == 0 else None)
                    if blk == 0:
                        statistic(squares)
                    base = hid_base + BLK * blk
                    with pe.Fori(0, KD // 2) as i:
                        for e in range(2):
                            out = accumulator(a0 + 24 * blk + BLK + e, 2 * i)
                            for half in range(2):
                                unit(u0 + 32 * blk + BLK + 2 * e + half, 4 * i, out, act_hi, act_lo, 8 * half,
                                     start=half == 0, stop=half == 1,
                                     tile_wait=(lambda k, f=half: pe.wait_ge(hid_lo_ready, base + 8 * f + k + 1))
                                     if e == 0 else None)

            mlp(U_MLP0, A_MLP0, 8, 0, 16)

            unit(U_SSM, 0, accumulator(A_SSM), xhi, xlo, 0,
                 tile_wait=lambda k: pe.wait_ge(xlo_ready, 16 + k + 1))
            statistic(24)
            unit(U_SSM + 1, 0, accumulator(A_SSM + 1), xhi, xlo, 0)
            pe.wait_ge(acc_drained, A_SSM + 1)
            for c in range(CHUNKS):
                last = pe.transpose(b_misc[:, P * c:P * c + P], tmp[:, 0, P * c:P * c + P], ident)
            last.then_inc(dtt_ready, 1)
            for j in (2, 3):
                unit(U_SSM + j, 0, accumulator(A_SSM + j), xhi, xlo, 0)
            pe.wait_ge(adt_ready, 1)
            flat = adt[:, :, :].rearrange("p c h -> p (c h)")
            pe.matmul(b_stat[:, 0:P], upper, flat, start=True, stop=True)
            pe.matmul(b_stat[:, P:2 * P], ones, flat, start=True, stop=True)
            for c in range(CHUNKS):
                last = pe.matmul(bank[2][0:HEADS, P * c:P * c + P], adt[:, c, :], upper, start=True, stop=True)
            last.then_inc(cum_ready, 1)
            for j in range(4, 7):
                unit(U_SSM + j, 0, accumulator(A_SSM + j), xhi, xlo, 0)

            def token_major(g):
                pe.wait_ge(silu_done, PER_GROUP * g + CONVS)
                pe.wait_ge(stat_drained, 3 + g)
                for c in range(CHUNKS):
                    for i in range(GT):
                        last = pe.transpose(XT_BANK[c][:, P * i:P * i + P], xact[:, i, P * c:P * c + P], ident)
                    last.then_inc(tok_ready, 1)
                for c in range(CHUNKS):
                    last = pe.transpose(b_misc[:, P * c:P * c + P], bf[:, P * c:P * c + P], ident)
                last.then_inc(tok_ready, 1)
                for c in range(CHUNKS):
                    last = pe.matmul(b_stat[:, P * c:P * c + P], bf[:, P * c:P * c + P],
                                     c_chunk(g, c), start=True, stop=True)
                last.then_inc(tok_ready, 1)

            def c_chunk(g, c):
                return cf[:, bass.ds(g, 1), P * c:P * c + P].rearrange("p a t -> p (a t)")

            def chunk(g, c):
                pe.wait_ge(m_ready, 4 * g + c + 1)
                if c:
                    pe.wait_ge(y_done, 4 * g + c)
                for hh in range(HPG):
                    last = pe.matmul(b_yd[64 * (hh % 2):64 * (hh % 2) + 64, P * (hh // 2):P * (hh // 2) + P],
                                     xdt[:, c, HD * hh:HD * hh + HD], mbuf[:, c % 2, P * hh:P * hh + P],
                                     start=True, stop=True)
                last.then_inc(yd_ready, 1)
                if c:
                    pe.wait_ge(state_ready, 3 * g + c)
                    for i in range(GT):
                        last = pe.matmul(b_yo[:, P * i:P * i + P], state[:, P * i:P * i + P], c_chunk(g, c),
                                         start=True, stop=True)
                    last.then_inc(yo_ready, 1)
                if c < CHUNKS - 1:
                    pe.wait_ge(dec_ready, 3 * g + c + 1)
                    pe.wait_ge(bt_ready, g + 1)
                    pe.matmul(b_st[:, :], bt[:, c, :], dec[:, c % 2, :], start=True, stop=True).then_inc(st_ready, 1)

            def group(g, r, last):
                for t in range(PER_GROUP + (2 if last else 0)):
                    if last and t >= GT:
                        unit(U_OUT + t - GT, 0, accumulator(A_OUT + t - GT), act_hi, act_lo, 0,
                             tile_wait=(lambda k: pe.wait_ge(ylo_ready, k + 1)) if t == GT else None)
                    else:
                        unit(U_GROUP + t, r, accumulator(A_SSM + 7 + t, r), xhi, xlo, 0)
                    if t == 0:
                        token_major(g)
                    if t in CHUNK_AFTER:
                        chunk(g, CHUNK_AFTER[t])
                    if t == 9:
                        statistic(24 + (GT - 1) * (g + 1))

            with pe.Fori(0, GROUPS - 1) as g:
                group(g, PER_GROUP * g, False)
            group(GROUPS - 1, PER_GROUP * (GROUPS - 1), True)
            for m in range(KD):
                unit(U_OUT + KD + m, 0, accumulator(A_OUT + KD + m), act_hi, act_lo, 8,
                     tile_wait=(lambda k: pe.wait_ge(ylo_ready, 8 + k + 1)) if m == 0 else None)

            mlp(U_MLP1, A_MLP1, 24, 32, 44)
            statistic(52)

        @block.vector
        def _(dve):
            steps = [0]

            def link(ins):
                steps[0] += 1
                ins.then_inc(chain, 1)
                dve.wait_ge(chain, steps[0])

            def residue(n, m):
                dve.wait_ge(xhi_ready, 8 * n + m + 1)
                tile = bass.ds(m, 1)
                dve.scalar_tensor_tensor(out=xlo[:, tile, :], in0=h[:, tile, :], scalar=col(gains[n], m),
                                         in1=xhi_f[:, tile, :], op0=ALU.mult, op1=ALU.subtract
                                         ).then_inc(xlo_ready, 1)

            def mean(k, buf, n):
                dve.wait_ge(stat_ready, k + 1)
                dve.tensor_scalar(buf[:, :], b_stat[:, :], 1.0 / n, EPS, ALU.mult, ALU.add
                                  ).then_inc(stat_drained, 1)

            def invert(k, buf, roots):
                if roots is None:
                    dve.wait_ge(stat_drained, k + 1)
                else:
                    dve.wait_ge(sqrt_done, roots)
                dve.reciprocal(buf[:, :], buf[:, :]).then_inc(recip_done, 1)
                dve.wait_ge(recip_done, k + 1)

            dve.wait_ge(params_landed, 16)
            for m in range(KD):
                dve.wait_ge(x_landed[m], 16)
                residue(0, m)
            mean(0, rstd, D_MODEL)
            invert(0, rstd, 1)
            dve.wait_ge(pads_clear, 4)
            dve.wait_ge(consts_landed, 16)
            for m in range(KD):
                gi, w = m // 2, WINDOWS[m // 2]
                dve.wait_ge(wt_used, gi + 1)
                dve.tensor_tensor(padded[0][:, PAD:], pool_acc[m][:, :], rstd[:, :], ALU.mult
                                  ).then_inc(acc_drained, 1)
                dve.wait_ge(acc_drained, m + 1)
                cur, span, slot = padded[0], 1, 1
                while span < w:
                    lo, nxt = 2 * span - 1, padded[slot]
                    link(dve.tensor_tensor(nxt[:, lo:], cur[:, lo:], cur[:, lo - span:PAD + TOK - span], ALU.add))
                    cur, span, slot = nxt, 2 * span, 3 - slot
                link(dve.scalar_tensor_tensor(out=mixed[:, :], in0=cur[:, PAD:], scalar=1.0 / w,
                                              in1=padded[0][:, PAD:], op0=ALU.mult, op1=ALU.subtract))
                link(dve.tensor_tensor(mixed[:, 0:PAD], cur[:, PAD:2 * PAD], inv_count[:, gi, :], ALU.mult))
                link(dve.tensor_tensor(mixed[:, 0:PAD], mixed[:, 0:PAD], padded[0][:, PAD:2 * PAD], ALU.subtract))
                link(dve.tensor_scalar(mixed[:, :], mixed[:, :], col("pool_b", m), col("pool_scale", m),
                                       ALU.add, ALU.mult))
                dve.tensor_tensor(h[:, m, :], h[:, m, :], mixed[:, :], ALU.add).then_inc(h_done, 1)
                if m:
                    residue(1, m - 1)
            residue(1, KD - 1)

            def mlp(u0, a0, hid_base, done, k, n_next):
                for blk in range(2):
                    with dve.Fori(0, BLK // 2) as i:
                        for e in range(2):
                            dve.wait_ge(wt_used, 2 * (u0 + 32 * blk + e + 1) + 4 * i)
                            count = hid_base + BLK * blk + e
                            a = a0 + 24 * blk + e
                            dve.tensor_scalar(tmp[:, e, :], acc[a % 2][:, :], 0.0, None, ALU.max
                                              ).then_inc(acc_drained, 1)
                            dve.wait_ge(acc_drained, a + 1 + 2 * i)
                            dve.tensor_tensor(tmp[:, e, :], tmp[:, e, :], tmp[:, e, :], ALU.mult
                                              ).then_inc(hid_sq_ready, 1)
                            dve.wait_ge(hid_hi_ready, count + 1 + 2 * i)
                            tile = bass.ds(2 * i + e, 1)
                            dve.tensor_tensor(act_lo[:, tile, :], tmp[:, e:e + 1, :], act_hi_f[:, tile, :],
                                              ALU.subtract).then_inc(hid_lo_ready, 1)
                    if blk == 0:
                        mean(k, rstd, D_MODEL)
                        invert(k, rstd, None)
                    with dve.Fori(0, KD // 2) as i:
                        for e in range(2):
                            dve.wait_ge(wt_used, 2 * (u0 + 32 * blk + BLK + 2 * e + 2) + 8 * i)
                            a = a0 + 24 * blk + BLK + e
                            tile = bass.ds(2 * i + e, 1)
                            dve.tensor_tensor(tmp[:, e, :], acc[a % 2][:, :], rstd[:, :], ALU.mult
                                              ).then_inc(acc_drained, 1)
                            dve.wait_ge(acc_drained, a + 1 + 2 * i)
                            dve.tensor_tensor(h[:, tile, :], h[:, tile, :], tmp[:, e:e + 1, :], ALU.add
                                              ).then_inc(h_done, 1)
                            if blk == 1 and n_next is not None:
                                residue(n_next, 2 * i + e)

            mlp(U_MLP0, A_MLP0, 0, 8, 1, 2)

            dve.wait_ge(wt_used, 2 * (U_SSM + 1))
            mean(2, rstd, D_MODEL)
            invert(2, rstd, 2)
            dve.tensor_tensor(tmp[:, 0, :], acc[A_SSM % 2][:, :], rstd[:, :], ALU.mult).then_inc(acc_drained, 1)

            def conv(g, q):
                c = U_SSM + 1 + q if isinstance(g, int) and g == 0 else U_GROUP + GT + q
                r = 0 if isinstance(g, int) and g == 0 else PER_GROUP * (g - 1)
                a, n = A_SSM + c - U_SSM, CONVS * g + q
                if c > U_SSM + 1:
                    dve.wait_ge(conv_ready, n)
                dve.wait_ge(wt_used, 2 * (c + 1) + 2 * r)
                dve.tensor_tensor(pre[:, CONV_K - 1:], acc[a % 2][:, :], rstd[:, :], ALU.mult
                                  ).then_inc(acc_drained, 1)
                dve.wait_ge(acc_drained, a + 1 + r)
                j = c - U_SSM
                if j >= 3:
                    dve.wait_ge(silu_done, j - 2 + r)
                if j == 2:
                    dve.wait_ge(dtt_ready, 1)
                out = tmp[:, j % 2, :]
                dve.tensor_scalar(out, pre[:, CONV_K - 1:], col("conv_w", 24 * (CONV_K - 1) + n),
                                  col("conv_b", n), ALU.mult, ALU.add).then_inc(conv_step, 1)
                for k in range(CONV_K - 2, -1, -1):
                    dve.wait_ge(conv_step, 3 * n + CONV_K - 1 - k)
                    tap = dve.scalar_tensor_tensor(out=out, in0=pre[:, k:k + TOK], scalar=col("conv_w", 24 * k + n),
                                                   in1=out, op0=ALU.mult, op1=ALU.add)
                    tap.then_inc(conv_ready if k == 0 else conv_step, 1)

            conv(0, 0)
            dve.wait_ge(dtt_ready, 1)
            bias = col("dt_bias", 0, HEADS).unsqueeze(1).to_broadcast(hd4)
            dt_raw = b_misc[:, :].rearrange("p (c n) -> p c n", c=CHUNKS)[:, :, P - HEADS:]
            link(dve.tensor_tensor(dtx[:, :, :], dt_raw, bias, ALU.add))
            dve.scalar_tensor_tensor(out=neg_abs[:, :, :], in0=dtx[:, :, :], scalar=-1.0, in1=dtx[:, :, :],
                                     op0=ALU.mult, op1=ALU.min).then_inc(dt_na, 1)
            link(dve.tensor_scalar(mx[:, :, :], dtx[:, :, :], 0.0, None, ALU.max))
            dve.wait_ge(dt_exp, 2)
            link(dve.tensor_scalar(rc[:, :, :], ex[:, :, :], 2.0, None, ALU.add))
            link(dve.reciprocal(rc[:, :, :], rc[:, :, :]))
            link(dve.tensor_tensor(ex[:, :, :], ex[:, :, :], rc[:, :, :], ALU.mult))
            link(dve.tensor_tensor(s2[:, :, :], ex[:, :, :], ex[:, :, :], ALU.mult))
            link(dve.tensor_scalar(ser[:, :, :], s2[:, :, :], 1.0 / (2 * N_SOFT + 1), None, ALU.mult))
            for n in range(N_SOFT - 1, 0, -1):
                link(dve.scalar_tensor_tensor(out=ser[:, :, :], in0=ser[:, :, :], scalar=1.0 / (2 * n + 1),
                                              in1=s2[:, :, :], op0=ALU.add, op1=ALU.mult))
            link(dve.scalar_tensor_tensor(out=ser[:, :, :], in0=ser[:, :, :], scalar=1.0, in1=ex[:, :, :],
                                          op0=ALU.add, op1=ALU.mult))
            link(dve.scalar_tensor_tensor(out=dt_t[:, :, :], in0=ser[:, :, :], scalar=2.0, in1=mx[:, :, :],
                                          op0=ALU.mult, op1=ALU.add))
            dve.scalar_tensor_tensor(out=adt[:, :, :], in0=dt_t[:, :, :], scalar=-1.0,
                                     in1=exp_a[:, :].unsqueeze(1).to_broadcast(hd4), op0=ALU.mult, op1=ALU.mult
                                     ).then_inc(adt_ready, 1)
            conv(0, 1)
            conv(0, 2)
            dve.wait_ge(cum_ready, 1)
            link(dve.tensor_copy(cum[:, :, :], b_stat[:, 0:2 * P].rearrange("p (a n) -> p a n", a=2)))
            dve.tensor_tensor(dend[:, :], cum[:, 1, :], cum[:, 0, :], ALU.subtract).then_inc(dend_in, 1)
            dve.tensor_copy(acs_f[:, :], bank[2][0:HEADS, :]).then_inc(acsf_ready, 1)
            for q in range(3, CONVS):
                conv(0, q)

            heads3 = [P, HPG, HD]

            def by_head(ap):
                return ap.rearrange("p (h d) -> p h d", h=HPG)

            def of_group(t, c, g, n):
                return t[:, bass.ds(HEADS * c + HPG * g, HPG)].unsqueeze(2).to_broadcast([P, HPG, n])

            def y_chunk(g, c):
                return yx[:, bass.ds(GT * g, GT), P * c:P * c + P]

            def tiles(ap):
                return ap.rearrange("p (i t) -> p i t", i=GT)

            def segment(g, c):
                dve.wait_ge(m_landed[c % 2], 16 * (c // 2 + 1) + 32 * g)
                m = by_head(mbuf[:, c % 2, :])
                dve.tensor_tensor(m, m, of_group(acs_t, c, g, P), ALU.subtract).then_inc(seg_step, 1)
                dve.wait_ge(seg_step, 4 * g + c + 1)
                dve.tensor_scalar(m, m, 0.0, None, ALU.min).then_inc(seg_ready, 1)

            def decay_times_cb(g, c):
                dve.wait_ge(exp_done, 4 * g + c + 1)
                m = by_head(mbuf[:, c % 2, :])
                dve.tensor_tensor(m, m, cbm[:, c:c + 1, :].to_broadcast([P, HPG, P]), ALU.mult
                                  ).then_inc(m_ready, 1)

            def add_y(g, c):
                if c == 0:
                    dve.wait_ge(skip_ready, GT * g + GT)
                dve.wait_ge(yd_ready, 4 * g + c + 1)
                y = y_chunk(g, c)
                first = dve.tensor_tensor(y, y, tiles(b_yd[:, :]), ALU.add)
                if c == 0:
                    first.then_inc(y_done, 1)
                    return
                first.then_inc(y_step, 1)
                dve.wait_ge(yo_ready, 3 * g + c)
                dve.wait_ge(e_landed[c % 2], 32 * (c // 2 + 1) + 64 * g if c % 2 else 32 + 32 * g)
                if True:
                    dve.tensor_tensor(tiles(ytmp[:, :]), tiles(b_yo[:, :]), e2[:, c % 2, :, :], ALU.mult
                                      ).then_inc(y_step, 1)
                dve.wait_ge(y_step, 6 * g + 2 * c)
                dve.tensor_tensor(y, y, tiles(ytmp[:, :]), ALU.add).then_inc(y_done, 1)

            def update_state(g, c):
                dve.wait_ge(st_ready, 3 * g + c + 1)
                if c == 0:
                    dve.tensor_copy(state[:, :], b_st[:, :]).then_inc(state_ready, 1)
                    return
                dve.wait_ge(state_ready, 3 * g + c)
                dve.tensor_tensor(by_head(state[:, :]), by_head(state[:, :]), of_group(cd, c, g, HD), ALU.mult
                                  ).then_inc(h_step, 1)
                dve.wait_ge(h_step, 2 * g + c)
                dve.tensor_tensor(state[:, :], state[:, :], b_st[:, :], ALU.add).then_inc(state_ready, 1)

            def token_major(g):
                for c in range(CHUNKS):
                    dve.wait_ge(tok_ready, 6 * g + c + 1)
                    dve.tensor_tensor(by_head(xdt[:, c, :]), by_head(XT_BANK[c][:, :]),
                                      of_group(dt_t[:, :, :].rearrange("p c h -> p (c h)"), c, g, HD), ALU.mult
                                      ).then_inc(xdt_ready, 1)
                dve.wait_ge(tok_ready, 6 * g + 6)
                dve.tensor_tensor(cbm[:, :, :], b_stat[:, :].rearrange("p (c t) -> p c t", c=CHUNKS),
                                  upper.unsqueeze(1).to_broadcast([P, CHUNKS, P]), ALU.mult).then_inc(cbm_ready, 1)

            def group(g, r, last):
                for t in range(PER_GROUP + (2 if last else 0)):
                    if t in (2, 3, 5, 6):
                        segment(g, {2: 0, 3: 1, 5: 2, 6: 3}[t])
                    if t < GT:
                        a = A_SSM + 7 + t
                        dve.wait_ge(wt_used, 2 * (U_GROUP + t + 1) + 2 * r)
                        dve.wait_ge(silu_done, 7 + t - 2 + r)
                        dve.tensor_tensor(tmp[:, (7 + t) % 2, :], acc[a % 2][:, :], rstd[:, :], ALU.mult
                                          ).then_inc(acc_drained, 1)
                    elif last:
                        add_output(t - GT)
                    else:
                        conv(g + 1, t - GT)
                    if t == 0:
                        token_major(g)
                    if t == 2:
                        dve.wait_ge(cbm_ready, g + 1)
                        decay_times_cb(g, 0)
                    if t == 3:
                        add_y(g, 0)
                        update_state(g, 0)
                        decay_times_cb(g, 1)
                    if t == 4:
                        add_y(g, 1)
                        update_state(g, 1)
                    if t == 5:
                        decay_times_cb(g, 2)
                    if t == 6:
                        add_y(g, 2)
                        update_state(g, 2)
                        decay_times_cb(g, 3)
                    if t == 7:
                        add_y(g, 3)
                        dve.wait_ge(y_done, 4 * g + 4)
                        y = yx[:, bass.ds(GT * g, GT), :]
                        dve.tensor_tensor(y, y, zs[:, bass.ds(GT * g, GT), :], ALU.mult).then_inc(gated, 1)
                    if t == 9:
                        mean(3 + g, rg, D_INNER // GROUPS)
                        invert(3 + g, rg, 3 + g)
                        for i in range(GT):
                            tile = bass.ds(GT * g + i, 1)
                            y = yx[:, tile, :]
                            dve.scalar_tensor_tensor(out=y, in0=y, scalar=col("norm_g", GT * g + i),
                                                     in1=rg[:, :].unsqueeze(1), op0=ALU.mult, op1=ALU.mult
                                                     ).then_inc(yn_ready, 1)
                            dve.wait_ge(yn_ready, GT * g + i + 1)
                            dve.tensor_scalar(act_hi[:, tile, :], y, 1.0, None, ALU.mult).then_inc(yhi_ready, 1)

            def add_output(n):
                a, m = A_OUT + n, n % KD
                dve.wait_ge(wt_used, 2 * (U_OUT + n + 1))
                dve.tensor_tensor(h[:, m, :], h[:, m, :], acc[a % 2][:, :], ALU.add).then_inc(acc_drained, 1)

            with dve.Fori(0, GROUPS - 1) as g:
                group(g, PER_GROUP * g, False)
            group(GROUPS - 1, PER_GROUP * (GROUPS - 1), True)
            for m in range(KD):
                add_output(KD + m)
                residue(3, m)

            mlp(U_MLP1, A_MLP1, 32, 24, 7, None)
            mean(8, rstd, D_MODEL)
            invert(8, rstd, 7)
            for m in range(KD):
                if m % 3 != 2:
                    dve.wait_ge(hg_ready, m + 1)
                    dve.tensor_tensor(hg[:, m, :], hg[:, m, :], rstd[:, :], ALU.mult).then_inc(out_ready, 1)


def kernel(**inputs):
    import numpy as np
    import concourse.bacc as bacc
    from concourse.bass_utils import run_bass_kernel_spmd

    a = {k: np.asarray(v) for k, v in inputs.items()}

    def units(w, k_tiles=8):
        k, n = w.shape
        t = w.reshape(k // (P * k_tiles), k_tiles, P, n // P, P)
        return t.transpose(3, 0, 2, 1, 4).reshape(-1, P, k_tiles * P)

    def mlp(i):
        w1, w2 = a["mlp_w1"][i], a["mlp_w2"][i]
        parts = []
        for blk in range(2):
            cols = slice(blk * BLK * P, (blk + 1) * BLK * P)
            parts += [units(w1[:, cols]), units(w2[cols, :])]
        return parts

    pw = a["pool_w"][0].reshape(2, 2, 2, P, 2, P)
    pool = pw.transpose(0, 3, 1, 4, 2, 5).reshape(2, P, 8 * P)
    w_in = a["ssm_w_in"][0]
    z0, x0, b0, c0 = 0, D_INNER, 2 * D_INNER, 2 * D_INNER + GROUPS * P
    gw = GT * P

    def conv_cols(g):
        return np.r_[b0 - x0 + g * P:b0 - x0 + (g + 1) * P, c0 - x0 + g * P:c0 - x0 + (g + 1) * P,
                     g * gw:(g + 1) * gw]

    ssm = [units(w_in[:, -P:]), units(w_in[:, x0 + conv_cols(0)])]
    for g in range(GROUPS):
        ssm.append(units(w_in[:, z0 + g * gw:z0 + (g + 1) * gw]))
        if g + 1 < GROUPS:
            ssm.append(units(w_in[:, x0 + conv_cols(g + 1)]))
    w_out = a["ssm_w_out"][0]
    out = [units(w_out[:1024]), units(w_out[1024:])]
    weights = np.concatenate([pool, *mlp(0), *ssm, *out, *mlp(1)])
    assert weights.shape[0] == UNITS

    def tiles(v):
        return v.reshape(-1, P).T

    channels = np.concatenate([conv_cols(g) for g in range(GROUPS)])
    rows = lambda v: np.broadcast_to(v, (P, v.shape[-1]))
    table = {
        "g0": tiles(a["norm_mix_g"][0]), "g1": tiles(a["norm_mlp_g"][0]),
        "g2": tiles(a["norm_mix_g"][1]), "g3": tiles(a["norm_mlp_g"][1]), "gf": tiles(a["final_g"]),
        "pool_b": tiles(a["pool_b"][0]), "pool_scale": tiles(a["pool_scale"][0]),
        "conv_w": np.concatenate([tiles(a["ssm_conv_w"][0][k][channels]) for k in range(CONV_K)], axis=1),
        "conv_b": tiles(a["ssm_conv_b"][0][channels]), "norm_g": tiles(a["ssm_norm_g"][0]),
        "skip": tiles(np.repeat(a["ssm_d"][0], HD)),
        "dt_bias": rows(a["ssm_dt_bias"][0]), "a_log": rows(a["ssm_a_log"][0]),
    }
    params = np.concatenate([table[k] for k in COLS], axis=1)
    inv_count = np.stack([1.0 / np.minimum(np.arange(PAD) + 1, w) for w in WINDOWS])
    consts = np.concatenate([np.ones((P, P)), np.triu(np.ones((P, P))), np.eye(P),
                             np.broadcast_to(inv_count.reshape(1, -1), (P, 4 * PAD))], axis=1).astype(np.float32)
    arrays = {"xt": a["x"][0].T.reshape(KD, P, TOK), "weights": weights, "params": params, "consts": consts}
    arrays = {k: np.ascontiguousarray(v) for k, v in arrays.items()}

    nc = bacc.Bacc("TRN2", target_bir_lowering=False, num_devices=1)
    args = [nc.dram_tensor(k, list(v.shape), F32, kind="ExternalInput").ap() for k, v in arrays.items()]
    out_t = nc.dram_tensor("out_t", [KD, P, TOK], F32, kind="ExternalOutput").ap()
    build(nc, *args, out_t)
    r = run_bass_kernel_spmd(nc, [arrays], core_ids=[0])
    return np.ascontiguousarray(r.results[0]["out_t"].reshape(D_MODEL, TOK).T)[None]
```

```python
from contextlib import ExitStack

import concourse.bass as bass
from concourse import mybir
from concourse.alu_op_type import AluOpType as ALU

F32 = mybir.dt.float32
F32R = mybir.dt.float32r
BF16 = mybir.dt.bfloat16
ACT = mybir.ActivationFunctionType

P = 128
TOK = 512
D_MODEL = 1024
KD = D_MODEL // P
D_FF = 4096
WINDOWS = (2, 4, 8, 16)
REACH = 16
HEADS, HD, GROUPS, CHUNKS, CONV_K = 32, 64, 4, 4, 4
HPG = HEADS // GROUPS
GT = HPG * HD // P
D_INNER = HEADS * HD
CONVS = GT + 2
EPS = 1e-5
N_SOFT = 7

U_POOL = 0
U_MLP0 = 2
BLK = 16
U_SSM = U_MLP0 + 64
U_GROUP = U_SSM + 7
PER_GROUP = GT + CONVS
U_OUT = U_SSM + 1 + 4 * PER_GROUP
U_MLP1 = U_OUT + 16
UNITS = U_MLP1 + 64
A_MLP0 = 2
A_SSM = A_MLP0 + 48
A_OUT = A_SSM + 1 + 4 * PER_GROUP
A_MLP1 = A_OUT + 16
COLS = {}
_at = 0
for _name, _n in (("g0", 8), ("g1", 8), ("g2", 8), ("g3", 8), ("gf", 8), ("pool_b", 8),
                  ("pool_scale", 8), ("conv_w", 96), ("conv_b", 24), ("norm_g", 16), ("skip", 16),
                  ("dt_bias", 32), ("a_log", 32)):
    COLS[_name] = _at
    _at += _n
N_PARAMS = _at
CHUNK_AFTER = {2: 0, 4: 1, 6: 2, 8: 3}
CHUNK_AFTER_LAST = {2: 0, 4: 1, 5: 2, 6: 3}


def build(nc, xt, x_tok, pooling, weights, params, consts, out_t):
    ctx = ExitStack()
    with ctx:
        sem = lambda name: ctx.enter_context(nc.semaphore(name))
        at = [nc.sbuf_base + 63 & ~63]

        def sb(name, shape, dtype=F32, offset=None):
            size = 4
            for n in shape[1:]:
                size *= n
            where = at[0] if offset is None else offset
            if offset is None:
                at[0] += size + 31 & ~31
            t = nc.alloc_sbuf_tensor_at(name, shape, dtype, offset=where)
            return t, where

        h, _ = sb("residual", [P, KD, TOK])
        xhi, _ = sb("x_hi", [P, KD, TOK], F32R)
        xhi_f = xhi[:, :, :].bitcast(F32)
        xlo, o_xlo = sb("x_lo", [P, KD, TOK], F32R)
        hg, _ = sb("scaled_residual", [P, KD, TOK], F32, o_xlo)
        act_hi, o_hi = sb("act_hi", [P, BLK, TOK], F32R)
        act_hi_f = act_hi[:, :, :].bitcast(F32)
        act_lo, o_lo = sb("act_lo", [P, BLK, TOK], F32R)
        yx, _ = sb("y_accumulated", [P, BLK, TOK], F32, o_lo)
        zs, _ = sb("z_silu", [P, BLK, TOK], F32, o_hi)
        xact, _ = sb("x_conv", [P, GT, TOK], F32, o_hi + 12 * TOK * 4)
        xn, _ = sb("x_token", [P, CHUNKS, D_MODEL], F32, o_hi)
        junk, _ = sb("x_token_squares", [P, D_MODEL], F32, o_lo)
        pools, _ = sb("pooling_matrices", [P, len(WINDOWS), 2 * (P + REACH)], F32, o_lo + 4 * D_MODEL)
        zeros, _ = sb("zeros", [P, TOK], BF16, o_lo + 4 * D_MODEL + 8 * len(WINDOWS) * (P + REACH))
        raw, _ = sb("w_raw", [P, 2, 1024])
        whi, _ = sb("w_hi", [P, 2, 1024], F32R)
        whi_f = whi[:, :, :].bitcast(F32)
        wlo, _ = sb("w_lo", [P, 2, 1024], F32R)
        prm, _ = sb("params", [P, N_PARAMS])
        cst, _ = sb("constants", [P, 3 * P])
        ones, upper, ident = (cst[:, i * P:(i + 1) * P] for i in range(3))
        r_tok, _ = sb("rstd_token", [P, CHUNKS])
        bias, _ = sb("pool_bias", [P, KD])
        tmp, _ = sb("tmp", [P, 2, TOK])
        sq, o_sq = sb("squares", [P, GT, TOK])
        ssq, _ = sb("square_sum", [P, TOK])
        rstd, _ = sb("rstd", [P, TOK])
        pre, _ = sb("conv_in", [P, CONV_K - 1 + TOK])
        bf, _ = sb("b_feature", [P, TOK])
        cf, _ = sb("c_feature", [P, GROUPS, TOK])
        xdt, _ = sb("x_dt", [P, CHUNKS, TOK])
        bt, _ = sb("b_token", [P, CHUNKS, P])
        cbm, _ = sb("cb_masked", [P, CHUNKS, P])
        dec, _ = sb("x_dt_decayed", [P, 2, TOK])
        mbuf, _ = sb("m", [P, 2, HPG * P])
        e2, _ = sb("decay_in", [P, 2, GT, P])
        state, _ = sb("state", [P, TOK])
        ytmp, _ = sb("y_tmp", [P, TOK])
        rg, _ = sb("group_rstd", [P, TOK])
        hd4 = [P, CHUNKS, HEADS]
        dtx, _ = sb("dt_x", hd4)
        neg_abs, _ = sb("dt_neg_abs", hd4)
        ex, _ = sb("dt_exp", hd4)
        mx, _ = sb("dt_max", hd4)
        rc, _ = sb("dt_rc", hd4)
        ser, _ = sb("dt_series", hd4)
        s2, _ = sb("dt_s2", hd4)
        dt_t, _ = sb("dt_token", hd4)
        adt, _ = sb("a_dt", hd4)
        exp_a, _ = sb("exp_a", [P, HEADS])
        cum, _ = sb("cumulated", [P, 2, CHUNKS * HEADS])
        acs_t = cum[:, 0, :]
        dend, _ = sb("decay_to_end", [P, CHUNKS * HEADS])
        cd, _ = sb("chunk_decay", [P, CHUNKS * HEADS])
        acs_f, _ = sb("a_cs_feature", [HEADS, TOK], F32, o_sq)
        eacs_f, _ = sb("exp_a_cs_feature", [HEADS, TOK], F32, o_sq + TOK * 4)
        assert at[0] <= nc.sbuf_usable_end, (at[0], nc.sbuf_usable_end)

        acs_dram = nc.dram_tensor("acs_scratch", [GROUPS, CHUNKS, HPG, P], F32).ap()
        eacs_dram = nc.dram_tensor("eacs_scratch", [GROUPS, CHUNKS, HPG, P], F32).ap()

        bank = [ctx.enter_context(nc.psum_tensor(f"bank{i}", [P, TOK], F32)) for i in range(8)]
        acc = bank[0:2]
        XT_BANK = (bank[2], bank[4], bank[5], bank[6])
        b_misc, b_yd, b_yo, b_st, b_stat = bank[3], bank[4], bank[5], bank[6], bank[7]

        x_landed = [sem(f"x_landed{m}") for m in range(KD)]
        xtok_landed = [sem(f"x_token_landed{c}") for c in range(CHUNKS)]
        pools_landed = sem("pooling_matrices_landed")
        sum_ready = sem("x_sums_ready")
        tok_mean = sem("x_mean_ready")
        tok_root = sem("x_root_ready")
        xn_ready = sem("x_token_normed")
        zeros_ready = sem("zeros_ready")
        mix_ready = sem("mix_ready")
        bias_ready = sem("pool_bias_ready")
        biased = sem("x_biased")
        biased_pool = sem("x_biased_pool")
        params_landed = sem("params_landed")
        consts_landed = sem("consts_landed")
        raw_landed = [sem("raw_landed0"), sem("raw_landed1")]
        hi_ready = sem("w_hi_ready")
        lo_ready = sem("w_lo_ready")
        wt_used = sem("w_used")
        acc_drained = sem("acc_drained")
        pool_added = sem("pool_added")
        h_done = sem("h_done")
        pooled_hi = sem("pooled_hi_ready")
        pooled_lo = sem("pooled_lo_ready")
        xhi_ready = sem("x_hi_ready")
        xlo_ready = sem("x_lo_ready")
        sq_ready = sem("sq_ready")
        ssq_added = sem("ssq_added")
        stat_ready = sem("stat_ready")
        stat_drained = sem("stat_drained")
        sqrt_done = sem("sqrt_done")
        recip_done = sem("recip_done")
        pads_clear = sem("pads_clear")
        chain = sem("dve_chain")
        hid_sq_ready = sem("hidden_square_ready")
        hid_hi_ready = sem("hidden_hi_ready")
        hid_lo_ready = sem("hidden_lo_ready")
        conv_step = sem("conv_step")
        conv_ready = sem("conv_ready")
        silu_done = sem("silu_done")
        skip_ready = sem("skip_ready")
        dtt_ready = sem("dt_transposed")
        dt_na = sem("dt_neg_abs_ready")
        dt_exp = sem("dt_exp_ready")
        adt_ready = sem("adt_ready")
        cum_ready = sem("cum_ready")
        acsf_ready = sem("acs_f_ready")
        dend_in = sem("decay_exponent_ready")
        decays = sem("decays_ready")
        scratch = sem("scratch_written")
        tok_ready = sem("token_major_ready")
        xdt_ready = sem("x_dt_ready")
        cbm_ready = sem("cb_ready")
        bt_ready = sem("b_token_ready")
        dec_ready = sem("dec_ready")
        m_landed = [sem("m_landed0"), sem("m_landed1")]
        e_landed = [sem("e_landed0"), sem("e_landed1")]
        seg_step = sem("segment_step")
        seg_ready = sem("segment_ready")
        exp_done = sem("exp_done")
        m_ready = sem("m_ready")
        yd_ready = sem("y_diag_ready")
        yo_ready = sem("y_off_ready")
        st_ready = sem("state_ready")
        y_step = sem("y_step")
        y_done = sem("y_done")
        h_step = sem("state_step")
        state_ready = sem("state_updated")
        gated = sem("gated")
        yn_ready = sem("y_normed")
        yhi_ready = sem("y_hi_ready")
        ylo_ready = sem("y_lo_ready")
        hg_ready = sem("scaled_ready")
        out_ready = sem("out_ready")
        out_ready_pool = sem("out_ready_pool")
        out_written = sem("out_written")

        def col(name, i, n=1):
            return prm[:, bass.ds(COLS[name] + i, n)]

        prep_from = [None, None, (h_done, 8), (acc_drained, A_OUT + 8), (h_done, 24)]
        gains = ["g0", "g1", "g2", "g3", "gf"]
        sq_base = [None, 0, 8, 32, 40]
        add_base = [None, 1, 10, 31, 40]
        stat_of = [None, 0, 1, 6, 7]
        SSM_SQ, SSM_ADD, SSM_STAT = 16, 18, 2

        block = ctx.enter_context(nc.Block())

        @block.sync
        def _(sp):
            def load_weights(c, r=0):
                if c >= 2:
                    sp.wait_ge(lo_ready, 2 * (c - 1) + 2 * r)
                sp.dma_start(raw[:, c % 2, :], weights[bass.ds(c + r, 1), :, :].rearrange("a p n -> (a p) n")
                             ).then_inc(raw_landed[c % 2], 16)

            def load_acs(g, c):
                sp.dma_start(mbuf[:, c % 2, :],
                             acs_dram[bass.ds(g, 1), c, :, :].rearrange("g h t -> g (h t)")
                             .to_broadcast([P, HPG * P])).then_inc(m_landed[c % 2], 16)

            def load_exp_acs(g, c):
                heads = eacs_dram[bass.ds(g, 1), c, :, :].rearrange("g (i two) t -> g two i t", two=2)
                for half in range(2):
                    sp.dma_start(e2[64 * half:64 * half + 64, c % 2, :, :],
                                 heads[:, half, :, :].to_broadcast([64, GT, P])).then_inc(e_landed[c % 2], 16)

            for c in range(CHUNKS):
                sp.dma_start(xn[:, c, :], x_tok[c, :, :]).then_inc(xtok_landed[c], 16)
            load_weights(0)
            for m in range(KD):
                if m == 2:
                    load_weights(1)
                sp.dma_start(h[:, m, :], xt[m, :, :]).then_inc(x_landed[m], 16)
            sp.dma_start(cst[:, :], consts).then_inc(consts_landed, 16)
            with sp.Fori(0, (U_GROUP - 1) // 2 - 1) as i:
                load_weights(2, 2 * i)
                load_weights(3, 2 * i)
            load_weights(U_GROUP - 1)
            load_weights(U_GROUP)
            sp.wait_ge(acsf_ready, 1)
            sp.wait_ge(decays, 3)
            for g in range(GROUPS):
                for src, dst in ((acs_f, acs_dram), (eacs_f, eacs_dram)):
                    sp.dma_start(dst[g].rearrange("c h t -> h c t"),
                                 src[g * HPG:(g + 1) * HPG, :].rearrange("h (c t) -> h c t", c=CHUNKS)
                                 ).then_inc(scratch, 16)
            load_weights(U_GROUP + 1)
            load_weights(U_GROUP + 2)
            sp.wait_ge(scratch, 2 * GROUPS * 16)
            load_acs(0, 0)

            def group_loads(g, r, first=False, last=False):
                after = {c: t for t, c in (CHUNK_AFTER_LAST if last else CHUNK_AFTER).items()}
                for t in range(PER_GROUP):
                    load_weights(U_GROUP + 3 + t, r)
                    if t == 0:
                        if not first:
                            sp.wait_ge(yd_ready, 4 * g)
                        load_acs(g, 1)
                    if t == 1:
                        if not first:
                            sp.wait_ge(y_done, 4 * g)
                        load_exp_acs(g, 1)
                        load_exp_acs(g, 2)
                    for c in (2, 3):
                        if t == after[c - 2] + 1:
                            sp.wait_ge(yd_ready, 4 * g + c - 1)
                            load_acs(g, c)
                    if t == after[1] + 2:
                        sp.wait_ge(y_done, 4 * g + 2)
                        load_exp_acs(g, 3)
                    if not last and t == after[2] + 1:
                        sp.wait_ge(yd_ready, 4 * g + 3)
                        load_acs(g + 1, 0)

            group_loads(0, 0, first=True)
            with sp.Fori(1, GROUPS - 1) as g:
                group_loads(g, PER_GROUP * g)
            group_loads(GROUPS - 1, PER_GROUP * (GROUPS - 1), last=True)
            rest = U_GROUP + 3 + 4 * PER_GROUP
            with sp.Fori(0, (UNITS - rest) // 2) as i:
                load_weights(rest, 2 * i)
                load_weights(rest + 1, 2 * i)
            for u in range(rest + (UNITS - rest) // 2 * 2, UNITS):
                load_weights(u)
            for m in range(KD):
                if m % 3 == 2:
                    sp.wait_ge(out_ready_pool, m // 3 + 1)
                else:
                    sp.wait_ge(out_ready, m - (m + 1) // 3 + 1)
                sp.dma_start(out_t[m, :, :], hg[:, m, :]).then_inc(out_written, 16)
            sp.wait_ge(out_written, 16 * KD)

        @block.scalar
        def _(act):
            act.dma_start(pools[:, :, :], pooling).then_inc(pools_landed, 16)
            act.dma_start(prm[:, :], params).then_inc(params_landed, 16)

            def round_half(c, half, r=0):
                if isinstance(r, int) and c + r >= UNITS:
                    return
                if half == 0:
                    act.wait_ge(raw_landed[c % 2], 16 * (c // 2 + 1) + 8 * r)
                if c >= 2:
                    act.wait_ge(wt_used, 2 * (c - 2) + half + 1 + 2 * r)
                part = slice(512 * half, 512 * half + 512)
                act.activation(whi[:, c % 2, part], raw[:, c % 2, part], ACT.Copy).then_inc(hi_ready, 1)

            def round_weights(c, r=0):
                round_half(c, 0, r)
                round_half(c, 1, r)

            def square(m, slot):
                act.activation(sq[:, slot, :], h[:, bass.ds(m, 1), :].rearrange("p a t -> p (a t)"),
                               ACT.Square).then_inc(sq_ready, 1)

            def prepare(n, m, slot, last=False):
                if slot is not None:
                    act.wait_ge(ssq_added, add_base[n] + m - 1)
                s, count = prep_from[n] if n > 1 else (acc_drained, 0) if m < 2 else (pool_added, -2)
                act.wait_ge(s, count + m + 1)
                if last:
                    act.activation(hg[:, bass.ds(m, 1), :], h[:, bass.ds(m, 1), :], ACT.Copy,
                                   scale=col(gains[n], m)).then_inc(hg_ready, 1)
                else:
                    act.activation(xhi[:, bass.ds(m, 1), :], h[:, bass.ds(m, 1), :], ACT.Copy,
                                   scale=col(gains[n], m)).then_inc(xhi_ready, 1)
                if slot is not None:
                    square(m, slot)

            def root(k, buf):
                act.wait_ge(stat_drained, k + 1)
                act.activation(buf[:, :], buf[:, :], ACT.Sqrt).then_inc(sqrt_done, 1)

            act.wait_ge(ssq_added, 1)
            act.activation(tmp[:, 0, 0:1], ssq[:, 0:1], ACT.Sqrt)
            for c in range(CHUNKS):
                act.wait_ge(xtok_landed[c], 16)
                act.activation(junk[:, :], xn[:, c, :], ACT.Square, accum_out=r_tok[:, c:c + 1]
                               ).then_inc(sum_ready, 1)
                act.wait_ge(tok_mean, c + 1)
                act.activation(r_tok[:, c:c + 1], r_tok[:, c:c + 1], ACT.Sqrt).then_inc(tok_root, 1)
            act.wait_ge(params_landed, 16)

            def pooled(m):
                act.wait_ge(mix_ready, m + 1)
                act.activation(xhi[:, m, :], bank[m][:, :], ACT.Copy, scale=col("g0", m)
                               ).then_inc(pooled_hi, 1)

            def add_bias(m):
                act.wait_ge(x_landed[m], 16)
                act.activation(h[:, m, :], h[:, m, :], ACT.Identity, bias=bias[:, m:m + 1]).then_inc(biased, 1)

            round_weights(0)
            for m in range(6):
                pooled(m)
            act.wait_ge(bias_ready, 1)
            add_bias(0)
            add_bias(1)
            round_weights(1)
            add_bias(2)
            add_bias(3)
            pooled(6)
            pooled(7)
            add_bias(4)
            prepare(1, 0, None)
            prepare(1, 1, None)
            round_half(2, 0)
            prepare(1, 2, None)
            prepare(1, 3, None)
            round_half(2, 1)
            for m in range(4, KD):
                prepare(1, m, None)
            round_weights(3)

            def mlp(u0, blk_base, n, n_next):
                for blk in range(2):
                    hid = blk_base + 16 * blk
                    with act.Fori(0, BLK // 2) as i:
                        for e in range(2):
                            round_weights(u0 + 32 * blk + e + 2, 2 * i)
                            if blk == 0 and e == 0:
                                act.wait_ge(ssq_added, add_base[n] + i)
                                square(i, 0)
                            act.wait_ge(hid_sq_ready, hid + e + 1 + 2 * i)
                            act.activation(act_hi[:, bass.ds(2 * i + e, 1), :], tmp[:, e:e + 1, :],
                                           ACT.Copy).then_inc(hid_hi_ready, 1)

                    def down(i, r):
                        for e in range(4):
                            round_weights(u0 + 32 * blk + BLK + e + 2, r)
                            if blk == 1 and e % 2:
                                prepare(n_next, 2 * i + e // 2, e // 2, n_next == 4)

                    with act.Fori(0, 3) as i:
                        down(i, 4 * i)
                    down(3, 12)

            mlp(U_MLP0, 0, 1, 2)

            def silu(dst, slot):
                act.activation(dst, tmp[:, slot:slot + 1, :], ACT.Silu).then_inc(silu_done, 1)

            def conv_silu(g, q):
                act.wait_ge(conv_ready, CONVS * g + q + 1)
                dst = (bf[:, :].unsqueeze(1) if q == 0 else cf[:, bass.ds(g, 1), :] if q == 1
                       else xact[:, q - 2:q - 1, :])
                silu(dst, (q + 1) % 2)
                if q >= 2:
                    act.wait_ge(silu_done, PER_GROUP * g + q + 1)
                    act.activation(yx[:, bass.ds(GT * g + q - 2, 1), :], xact[:, q - 2:q - 1, :], ACT.Copy,
                                   scale=col("skip", GT * g + q - 2)).then_inc(skip_ready, 1)

            round_weights(U_SSM + 2)
            root(1, rstd)
            act.activation(exp_a[:, :], col("a_log", 0, HEADS), ACT.Exp).then_inc(dt_exp, 1)
            round_weights(U_SSM + 3)
            act.wait_ge(dt_na, 1)
            act.activation(ex[:, :, :], neg_abs[:, :, :], ACT.Exp).then_inc(dt_exp, 1)
            for j in range(2, 7):
                round_half(U_SSM + 2 + j, 0)
                conv_silu(0, j - 2)
                round_half(U_SSM + 2 + j, 1)
                if j == 4:
                    act.wait_ge(dend_in, 1)
                    act.activation(dend[:, :], dend[:, :], ACT.Exp).then_inc(decays, 1)
                    act.activation(cd[:, :], cum[:, 1, :], ACT.Exp).then_inc(decays, 1)
                    act.wait_ge(acsf_ready, 1)
                    act.activation(eacs_f[:, :], acs_f[:, :], ACT.Exp).then_inc(decays, 1)

            def exp_segments(g, c):
                act.wait_ge(seg_ready, 4 * g + c + 1)
                act.activation(mbuf[:, c % 2, :], mbuf[:, c % 2, :], ACT.Exp).then_inc(exp_done, 1)

            def group_squares(g):
                act.wait_ge(gated, g + 1)
                for i in range(GT):
                    act.activation(sq[:, i:i + 1, :], yx[:, bass.ds(GT * g + i, 1), :],
                                   ACT.Square).then_inc(sq_ready, 1)

            def group(g, r, first=False, last=False):
                sched = CHUNK_AFTER_LAST if last else CHUNK_AFTER
                for t in range(PER_GROUP + (2 if last else 0)):
                    round_half(U_GROUP + t + 2, 0, r)
                    if t == 0:
                        conv_silu(g, CONVS - 1)
                    elif t <= GT:
                        z = t - 1
                        act.wait_ge(acc_drained, A_SSM + 8 + z + r)
                        if z == 0:
                            act.wait_ge(tok_ready, 6 * g + CHUNKS)
                        silu(zs[:, bass.ds(GT * g + z, 1), :], (z + 1) % 2)
                    elif not last:
                        conv_silu(g + 1, t - GT - 1)
                    if last and t == 8:
                        group_squares(g)
                    round_half(U_GROUP + t + 2, 1, r)
                    if t == 0:
                        act.wait_ge(tok_ready, 6 * g + CHUNKS + 1)
                        act.activation(bt[:, :, :], b_misc[:, :].rearrange("p (c n) -> p c n", c=CHUNKS),
                                       ACT.Copy).then_inc(bt_ready, 1)
                        if not first:
                            group_squares(g - 1)
                    if t + 1 in sched:
                        exp_segments(g, sched[t + 1])
                    if not first and t == 2:
                        root(SSM_STAT - 1 + g, rg)
                    if last and t == 9:
                        root(SSM_STAT + g, rg)

            group(0, 0, first=True)
            with act.Fori(1, GROUPS - 1) as g:
                group(g, PER_GROUP * g)
            group(GROUPS - 1, PER_GROUP * (GROUPS - 1), last=True)
            for m in range(KD):
                round_weights(U_OUT + 8 + m + 2)
                prepare(3, m, None)

            mlp(U_MLP1, 32, 3, 4)
            root(7, rstd)

        @block.gpsimd
        def _(pool):
            pool.memset(pre[:, 0:CONV_K - 1], 0.0).then_inc(pads_clear, 1)

            def split_half(c, half, r=0):
                if isinstance(r, int) and c + r >= UNITS:
                    return
                pool.wait_ge(hi_ready, 2 * c + half + 1 + 2 * r)
                part = slice(512 * half, 512 * half + 512)
                pool.tensor_tensor(wlo[:, c % 2, part], raw[:, c % 2, part], whi_f[:, c % 2, part],
                                   ALU.subtract).then_inc(lo_ready, 1)

            def split_weights(c, r=0):
                split_half(c, 0, r)
                split_half(c, 1, r)

            def clear_sum(n):
                if n > 1:
                    pool.wait_ge(stat_ready, stat_of[n])
                pool.memset(ssq[:, :], 0.0).then_inc(ssq_added, 1)

            def add_squares(n, m, slot):
                pool.wait_ge(sq_ready, sq_base[n] + m + 1)
                pool.wait_ge(ssq_added, add_base[n] + m)
                pool.tensor_tensor(ssq[:, :], ssq[:, :], sq[:, slot, :], ALU.add).then_inc(ssq_added, 1)

            clear_sum(1)

            split_weights(0)
            split_weights(1)
            pool.wait_ge(bias_ready, 1)
            for m in range(5, KD):
                pool.wait_ge(x_landed[m], 16)
                pool.tensor_tensor(h[:, m, :], h[:, m, :], bias[:, m:m + 1].to_broadcast([P, TOK]), ALU.add
                                   ).then_inc(biased_pool, 1)
            split_weights(2)
            split_weights(3)

            def mlp(u0, n, n_next):
                for blk in range(2):
                    with pool.Fori(0, BLK // 2) as i:
                        split_weights(u0 + 32 * blk + 2, 2 * i)
                        if blk == 0:
                            add_squares(n, i, 0)
                        split_weights(u0 + 32 * blk + 3, 2 * i)
                    if blk == 1:
                        clear_sum(n_next)

                    def down(i, r):
                        for e in range(4):
                            split_weights(u0 + 32 * blk + BLK + e + 2, r)
                            if blk == 1 and e % 2:
                                add_squares(n_next, 2 * i + e // 2, e // 2)

                    with pool.Fori(0, 3) as i:
                        down(i, 4 * i)
                    down(3, 12)

            mlp(U_MLP0, 1, 2)
            for j in range(7):
                split_weights(U_SSM + 2 + j)

            def decayed(g, c):
                pool.wait_ge(xdt_ready, 4 * g + c + 1)
                if c == 2:
                    pool.wait_ge(st_ready, 3 * g + 1)
                pool.tensor_tensor(
                    dec[:, c % 2, :].rearrange("p (h d) -> p h d", h=HPG),
                    xdt[:, c, :].rearrange("p (h d) -> p h d", h=HPG),
                    dend[:, bass.ds(HEADS * c + HPG * g, HPG)].unsqueeze(2).to_broadcast([P, HPG, HD]),
                    ALU.mult).then_inc(dec_ready, 1)

            def group_sum(g):
                pool.wait_ge(stat_ready, SSM_STAT + g)
                for i in range(1, GT):
                    pool.wait_ge(sq_ready, SSM_SQ + GT * g + i + 1)
                    if i > 1:
                        pool.wait_ge(ssq_added, SSM_ADD + (GT - 1) * g + i - 1)
                    pool.tensor_tensor(ssq[:, :], sq[:, 0, :] if i == 1 else ssq[:, :], sq[:, i, :],
                                       ALU.add).then_inc(ssq_added, 1)

            def y_residue(g, i):
                pool.wait_ge(yhi_ready, GT * g + i + 1)
                tile = bass.ds(GT * g + i, 1)
                pool.tensor_tensor(act_lo[:, tile, :], yx[:, tile, :], act_hi_f[:, tile, :],
                                   ALU.subtract).then_inc(ylo_ready, 1)

            def group(g, r, first=False, last=False):
                for t in range(PER_GROUP + (2 if last else 0)):
                    split_half(U_GROUP + 2 + t, 0, r)
                    if t == 1:
                        pool.wait_ge(decays, 1)
                        decayed(g, 0)
                        decayed(g, 1)
                    if t == 3:
                        decayed(g, 2)
                    if not first and t == 5:
                        y_residue(g - 1, 0)
                        y_residue(g - 1, 1)
                    split_half(U_GROUP + 2 + t, 1, r)
                    if not first and t == 1:
                        group_sum(g - 1)
                    if not first and t == (7 if last else 9):
                        y_residue(g - 1, 2)
                        y_residue(g - 1, 3)
                    if last and t == 8:
                        group_sum(g)
                    if last and t == 9:
                        for i in range(GT):
                            y_residue(g, i)

            group(0, 0, first=True)
            with pool.Fori(1, GROUPS - 1) as g:
                group(g, PER_GROUP * g)
            group(GROUPS - 1, PER_GROUP * (GROUPS - 1), last=True)
            clear_sum(3)
            for m in range(KD):
                split_weights(U_OUT + 8 + m + 2)
            mlp(U_MLP1, 3, 4)
            pool.wait_ge(recip_done, 8)
            for m in range(2, KD, 3):
                pool.wait_ge(hg_ready, m + 1)
                pool.tensor_tensor(hg[:, m, :], hg[:, m, :], rstd[:, :], ALU.mult).then_inc(out_ready_pool, 1)

        @block.tensor
        def _(pe):
            def three(out, wh, wl, xh, xl, start, stop):
                pe.matmul(out, wh, xh, start=start, stop=False)
                pe.matmul(out, wh, xl, start=False, stop=False)
                return pe.matmul(out, wl, xh, start=False, stop=stop)

            def unit(c, r, out, hi, lo, tile0, start=True, stop=True, tile_wait=None):
                for k in range(8):
                    if k % 4 == 0:
                        pe.wait_ge(lo_ready, 2 * c + k // 4 + 1 + 2 * r)
                    if tile_wait is not None:
                        tile_wait(k)
                    w = slice(P * k, P * k + P)
                    last = three(out, whi[:, c % 2, w], wlo[:, c % 2, w], hi[:, tile0 + k, :],
                                 lo[:, tile0 + k, :], start and k == 0, stop and k == 7)
                    if k % 4 == 3:
                        last.then_inc(wt_used, 1)

            def accumulator(a, r=0):
                pe.wait_ge(acc_drained, a - 1 + r)
                return acc[a % 2][:, :]

            def statistic(tiles):
                pe.wait_ge(ssq_added, tiles)
                pe.matmul(b_stat[:, :], ones, ssq[:, :], start=True, stop=True).then_inc(stat_ready, 1)

            pe.wait_ge(zeros_ready, 1)
            for m in range(2 * KD):
                pe.matmul(bank[m % KD][:, :], zeros[:, 0:P], zeros[:, :], start=m < KD, stop=False)
            pe.wait_ge(pools_landed, 16)
            for c in range(CHUNKS):
                n = P if c == CHUNKS - 1 else P + REACH
                for m in range(KD):
                    if m % 4 == 0:
                        pe.wait_ge(xn_ready, 2 * c + m // 4 + 1)
                    o = 0 if c == 0 else P + REACH
                    last = pe.matmul(bank[m][:, P * c:P * c + n], xn[:, c, P * m:P * m + P],
                                     pools[:, m // 2, o:o + n], start=False, stop=c == CHUNKS - 1)
                    if c == CHUNKS - 1:
                        last.then_inc(mix_ready, 1)

            def pool_maps(gi):
                pe.wait_ge(lo_ready, gi + 1)
                pe.wait_ge(pooled_lo, 2 * gi + 2)
                for mt in range(2):
                    for k in range(2):
                        w = bass.ds(512 * (gi % 2) + 256 * mt + 128 * k, P)
                        last = three(bank[2 * gi + mt][:, :], whi[:, gi // 2, w], wlo[:, gi // 2, w],
                                     xhi[:, 2 * gi + k, :], xlo[:, 2 * gi + k, :], k == 0, k == 1)
                last.then_inc(wt_used, 1)

            for gi in range(4):
                pool_maps(gi)

            def mlp(u0, a0, x_base, hid_base, squares):
                for blk in range(2):
                    with pe.Fori(0, BLK // 2) as i:
                        for e in range(2):
                            out = accumulator(a0 + 24 * blk + e, 2 * i)
                            unit(u0 + 32 * blk + e, 2 * i, out, xhi, xlo, 0,
                                 tile_wait=(lambda k: pe.wait_ge(xlo_ready, x_base + k + 1)) if e == 0 else None)
                    if blk == 0:
                        statistic(squares)
                    base = hid_base + BLK * blk
                    with pe.Fori(0, KD // 2) as i:
                        for e in range(2):
                            out = accumulator(a0 + 24 * blk + BLK + e, 2 * i)
                            for half in range(2):
                                unit(u0 + 32 * blk + BLK + 2 * e + half, 4 * i, out, act_hi, act_lo, 8 * half,
                                     start=half == 0, stop=half == 1,
                                     tile_wait=(lambda k, f=half: pe.wait_ge(hid_lo_ready, base + 8 * f + k + 1))
                                     if e == 0 else None)

            pe.wait_ge(consts_landed, 16)
            mlp(U_MLP0, A_MLP0, 0, 0, 9)

            unit(U_SSM, 0, accumulator(A_SSM), xhi, xlo, 0,
                 tile_wait=lambda k: pe.wait_ge(xlo_ready, 8 + k + 1))
            statistic(SSM_ADD)
            unit(U_SSM + 1, 0, accumulator(A_SSM + 1), xhi, xlo, 0)
            pe.wait_ge(acc_drained, A_SSM + 1)
            for c in range(CHUNKS):
                last = pe.transpose(b_misc[:, P * c:P * c + P], tmp[:, 0, P * c:P * c + P], ident)
            last.then_inc(dtt_ready, 1)
            for j in (2, 3):
                unit(U_SSM + j, 0, accumulator(A_SSM + j), xhi, xlo, 0)
            pe.wait_ge(adt_ready, 1)
            flat = adt[:, :, :].rearrange("p c h -> p (c h)")
            pe.matmul(b_stat[:, 0:P], upper, flat, start=True, stop=True)
            pe.matmul(b_stat[:, P:2 * P], ones, flat, start=True, stop=True)
            for c in range(CHUNKS):
                last = pe.matmul(bank[2][0:HEADS, P * c:P * c + P], adt[:, c, :], upper, start=True, stop=True)
            last.then_inc(cum_ready, 1)
            for j in range(4, 7):
                unit(U_SSM + j, 0, accumulator(A_SSM + j), xhi, xlo, 0)

            def token_major(g, first):
                pe.wait_ge(silu_done, PER_GROUP * g + CONVS)
                pe.wait_ge(stat_drained, SSM_STAT + g - (0 if first else 1))
                for c in range(CHUNKS):
                    for i in range(GT):
                        last = pe.transpose(XT_BANK[c][:, P * i:P * i + P], xact[:, i, P * c:P * c + P], ident)
                    last.then_inc(tok_ready, 1)
                for c in range(CHUNKS):
                    last = pe.transpose(b_misc[:, P * c:P * c + P], bf[:, P * c:P * c + P], ident)
                last.then_inc(tok_ready, 1)
                for c in range(CHUNKS):
                    last = pe.matmul(b_stat[:, P * c:P * c + P], bf[:, P * c:P * c + P],
                                     c_chunk(g, c), start=True, stop=True)
                last.then_inc(tok_ready, 1)

            def c_chunk(g, c):
                return cf[:, bass.ds(g, 1), P * c:P * c + P].rearrange("p a t -> p (a t)")

            def chunk(g, c):
                pe.wait_ge(m_ready, 4 * g + c + 1)
                if c:
                    pe.wait_ge(y_done, 4 * g + c)
                for hh in range(HPG):
                    last = pe.matmul(b_yd[64 * (hh % 2):64 * (hh % 2) + 64, P * (hh // 2):P * (hh // 2) + P],
                                     xdt[:, c, HD * hh:HD * hh + HD], mbuf[:, c % 2, P * hh:P * hh + P],
                                     start=True, stop=True)
                last.then_inc(yd_ready, 1)
                if c:
                    pe.wait_ge(state_ready, 3 * g + c)
                    for i in range(GT):
                        last = pe.matmul(b_yo[:, P * i:P * i + P], state[:, P * i:P * i + P], c_chunk(g, c),
                                         start=True, stop=True)
                    last.then_inc(yo_ready, 1)
                if c < CHUNKS - 1:
                    pe.wait_ge(dec_ready, 3 * g + c + 1)
                    pe.wait_ge(bt_ready, g + 1)
                    pe.matmul(b_st[:, :], bt[:, c, :], dec[:, c % 2, :], start=True, stop=True).then_inc(st_ready, 1)

            def group(g, r, first=False, last=False):
                sched = CHUNK_AFTER_LAST if last else CHUNK_AFTER
                for t in range(PER_GROUP + (2 if last else 0)):
                    if last and t >= GT:
                        unit(U_OUT + t - GT, 0, accumulator(A_OUT + t - GT), act_hi, act_lo, 0,
                             tile_wait=(lambda k: pe.wait_ge(ylo_ready, k + 1)) if t == GT else None)
                    else:
                        unit(U_GROUP + t, r, accumulator(A_SSM + 7 + t, r), xhi, xlo, 0)
                    if t == 0:
                        token_major(g, first)
                    if not first and t == 2:
                        pe.wait_ge(cbm_ready, g + 1)
                        statistic(SSM_ADD + (GT - 1) * g)
                    if t in sched:
                        chunk(g, sched[t])
                    if last and t == 9:
                        statistic(SSM_ADD + (GT - 1) * (g + 1))

            group(0, 0, first=True)
            with pe.Fori(1, GROUPS - 1) as g:
                group(g, PER_GROUP * g)
            group(GROUPS - 1, PER_GROUP * (GROUPS - 1), last=True)
            for m in range(KD):
                unit(U_OUT + KD + m, 0, accumulator(A_OUT + KD + m), act_hi, act_lo, 8,
                     tile_wait=(lambda k: pe.wait_ge(ylo_ready, 8 + k + 1)) if m == 0 else None)

            mlp(U_MLP1, A_MLP1, 16, 32, 39)
            statistic(48)

        @block.vector
        def _(dve):
            steps = [0]

            def link(ins):
                steps[0] += 1
                ins.then_inc(chain, 1)
                dve.wait_ge(chain, steps[0])

            def residue(n, m):
                dve.wait_ge(xhi_ready, 8 * (n - 1) + m + 1)
                tile = bass.ds(m, 1)
                dve.scalar_tensor_tensor(out=xlo[:, tile, :], in0=h[:, tile, :], scalar=col(gains[n], m),
                                         in1=xhi_f[:, tile, :], op0=ALU.mult, op1=ALU.subtract
                                         ).then_inc(xlo_ready, 1)

            def mean(k, buf, n):
                dve.wait_ge(stat_ready, k + 1)
                dve.tensor_scalar(buf[:, :], b_stat[:, :], 1.0 / n, EPS, ALU.mult, ALU.add
                                  ).then_inc(stat_drained, 1)

            def invert(k, buf, roots):
                if roots is None:
                    dve.wait_ge(stat_drained, k + 1)
                else:
                    dve.wait_ge(sqrt_done, roots)
                dve.reciprocal(buf[:, :], buf[:, :]).then_inc(recip_done, 1)

            dve.memset(zeros[:, :], 0.0).then_inc(zeros_ready, 1)
            for c in range(CHUNKS):
                r = r_tok[:, c:c + 1]
                dve.wait_ge(sum_ready, c + 1)
                dve.tensor_scalar(r, r, 1.0 / D_MODEL, EPS, ALU.mult, ALU.add).then_inc(tok_mean, 1)
                dve.wait_ge(tok_root, c + 1)
                link(dve.reciprocal(r, r))
                for half in range(2):
                    part = xn[:, c, 512 * half:512 * half + 512]
                    dve.tensor_scalar(part, part, r, None, ALU.mult).then_inc(xn_ready, 1)
                if c == 0:
                    dve.wait_ge(params_landed, 16)
                    dve.tensor_tensor(bias[:, :], col("pool_b", 0, KD), col("pool_scale", 0, KD), ALU.mult
                                      ).then_inc(bias_ready, 1)

            def pooled_residue(m):
                dve.wait_ge(pooled_hi, m + 1)
                dve.scalar_tensor_tensor(out=xlo[:, m, :], in0=bank[m][:, :], scalar=col("g0", m),
                                         in1=xhi_f[:, m, :], op0=ALU.mult, op1=ALU.subtract
                                         ).then_inc(pooled_lo, 1)

            def add_pooled(m):
                dve.wait_ge(wt_used, m // 2 + 1)
                if m < 5:
                    dve.wait_ge(biased, m + 1)
                else:
                    dve.wait_ge(biased_pool, m - 4)
                dve.scalar_tensor_tensor(out=h[:, m, :], in0=bank[m][:, :], scalar=col("pool_scale", m),
                                         in1=h[:, m, :], op0=ALU.mult, op1=ALU.add
                                         ).then_inc(acc_drained if m < 2 else pool_added, 1)

            for m in range(4):
                pooled_residue(m)
            for m in (0, 2):
                pooled_residue(m + 4)
                pooled_residue(m + 5)
                add_pooled(m)
                add_pooled(m + 1)
            for m in (4, 6):
                residue(1, m - 4)
                residue(1, m - 3)
                add_pooled(m)
                add_pooled(m + 1)
            for m in range(4, KD):
                residue(1, m)

            def mlp(u0, a0, hid_base, k, n_next):
                for blk in range(2):
                    with dve.Fori(0, BLK // 2) as i:
                        for e in range(2):
                            dve.wait_ge(wt_used, 2 * (u0 + 32 * blk + e + 1) + 4 * i)
                            count = hid_base + BLK * blk + e
                            a = a0 + 24 * blk + e
                            dve.tensor_scalar(tmp[:, e, :], acc[a % 2][:, :], 0.0, None, ALU.max
                                              ).then_inc(acc_drained, 1)
                            dve.wait_ge(acc_drained, a + 1 + 2 * i)
                            dve.tensor_tensor(tmp[:, e, :], tmp[:, e, :], tmp[:, e, :], ALU.mult
                                              ).then_inc(hid_sq_ready, 1)
                            dve.wait_ge(hid_hi_ready, count + 1 + 2 * i)
                            tile = bass.ds(2 * i + e, 1)
                            dve.tensor_tensor(act_lo[:, tile, :], tmp[:, e:e + 1, :], act_hi_f[:, tile, :],
                                              ALU.subtract).then_inc(hid_lo_ready, 1)
                    if blk == 0:
                        mean(k, rstd, D_MODEL)
                        invert(k, rstd, None)
                        dve.wait_ge(recip_done, k + 1)
                    with dve.Fori(0, KD // 2) as i:
                        for e in range(2):
                            dve.wait_ge(wt_used, 2 * (u0 + 32 * blk + BLK + 2 * e + 2) + 8 * i)
                            a = a0 + 24 * blk + BLK + e
                            tile = bass.ds(2 * i + e, 1)
                            dve.tensor_tensor(tmp[:, e, :], acc[a % 2][:, :], rstd[:, :], ALU.mult
                                              ).then_inc(acc_drained, 1)
                            dve.wait_ge(acc_drained, a + 1 + 2 * i)
                            dve.tensor_tensor(h[:, tile, :], h[:, tile, :], tmp[:, e:e + 1, :], ALU.add
                                              ).then_inc(h_done, 1)
                            if blk == 1 and n_next is not None:
                                residue(n_next, 2 * i + e)

            mlp(U_MLP0, A_MLP0, 0, 0, 2)

            dve.wait_ge(wt_used, 2 * (U_SSM + 1))
            mean(1, rstd, D_MODEL)
            invert(1, rstd, 1)
            dve.wait_ge(recip_done, 2)
            dve.tensor_tensor(tmp[:, 0, :], acc[A_SSM % 2][:, :], rstd[:, :], ALU.mult).then_inc(acc_drained, 1)

            def conv(g, q):
                c = U_SSM + 1 + q if isinstance(g, int) and g == 0 else U_GROUP + GT + q
                r = 0 if isinstance(g, int) and g == 0 else PER_GROUP * (g - 1)
                a, n = A_SSM + c - U_SSM, CONVS * g + q
                if c > U_SSM + 1:
                    dve.wait_ge(conv_ready, n)
                dve.wait_ge(wt_used, 2 * (c + 1) + 2 * r)
                dve.tensor_tensor(pre[:, CONV_K - 1:], acc[a % 2][:, :], rstd[:, :], ALU.mult
                                  ).then_inc(acc_drained, 1)
                dve.wait_ge(acc_drained, a + 1 + r)
                j = c - U_SSM
                if j >= 3:
                    dve.wait_ge(silu_done, j - 2 + r)
                if j == 2:
                    dve.wait_ge(dtt_ready, 1)
                out = tmp[:, j % 2, :]
                dve.tensor_scalar(out, pre[:, CONV_K - 1:], col("conv_w", 24 * (CONV_K - 1) + n),
                                  col("conv_b", n), ALU.mult, ALU.add).then_inc(conv_step, 1)
                for k in range(CONV_K - 2, -1, -1):
                    dve.wait_ge(conv_step, 3 * n + CONV_K - 1 - k)
                    tap = dve.scalar_tensor_tensor(out=out, in0=pre[:, k:k + TOK], scalar=col("conv_w", 24 * k + n),
                                                   in1=out, op0=ALU.mult, op1=ALU.add)
                    tap.then_inc(conv_ready if k == 0 else conv_step, 1)

            dve.wait_ge(consts_landed, 16)
            dve.wait_ge(pads_clear, 1)
            conv(0, 0)
            dve.wait_ge(dtt_ready, 1)
            dt_bias = col("dt_bias", 0, HEADS).unsqueeze(1).to_broadcast(hd4)
            dt_raw = b_misc[:, :].rearrange("p (c n) -> p c n", c=CHUNKS)[:, :, P - HEADS:]
            link(dve.tensor_tensor(dtx[:, :, :], dt_raw, dt_bias, ALU.add))
            dve.scalar_tensor_tensor(out=neg_abs[:, :, :], in0=dtx[:, :, :], scalar=-1.0, in1=dtx[:, :, :],
                                     op0=ALU.mult, op1=ALU.min).then_inc(dt_na, 1)
            link(dve.tensor_scalar(mx[:, :, :], dtx[:, :, :], 0.0, None, ALU.max))
            dve.wait_ge(dt_exp, 2)
            link(dve.tensor_scalar(rc[:, :, :], ex[:, :, :], 2.0, None, ALU.add))
            link(dve.reciprocal(rc[:, :, :], rc[:, :, :]))
            link(dve.tensor_tensor(ex[:, :, :], ex[:, :, :], rc[:, :, :], ALU.mult))
            link(dve.tensor_tensor(s2[:, :, :], ex[:, :, :], ex[:, :, :], ALU.mult))
            link(dve.tensor_scalar(ser[:, :, :], s2[:, :, :], 1.0 / (2 * N_SOFT + 1), None, ALU.mult))
            for n in range(N_SOFT - 1, 0, -1):
                link(dve.scalar_tensor_tensor(out=ser[:, :, :], in0=ser[:, :, :], scalar=1.0 / (2 * n + 1),
                                              in1=s2[:, :, :], op0=ALU.add, op1=ALU.mult))
            link(dve.scalar_tensor_tensor(out=ser[:, :, :], in0=ser[:, :, :], scalar=1.0, in1=ex[:, :, :],
                                          op0=ALU.add, op1=ALU.mult))
            link(dve.scalar_tensor_tensor(out=dt_t[:, :, :], in0=ser[:, :, :], scalar=2.0, in1=mx[:, :, :],
                                          op0=ALU.mult, op1=ALU.add))
            dve.scalar_tensor_tensor(out=adt[:, :, :], in0=dt_t[:, :, :], scalar=-1.0,
                                     in1=exp_a[:, :].unsqueeze(1).to_broadcast(hd4), op0=ALU.mult, op1=ALU.mult
                                     ).then_inc(adt_ready, 1)
            conv(0, 1)
            conv(0, 2)
            dve.wait_ge(cum_ready, 1)
            link(dve.tensor_copy(cum[:, :, :], b_stat[:, 0:2 * P].rearrange("p (a n) -> p a n", a=2)))
            dve.tensor_tensor(dend[:, :], cum[:, 1, :], cum[:, 0, :], ALU.subtract).then_inc(dend_in, 1)
            dve.tensor_copy(acs_f[:, :], bank[2][0:HEADS, :]).then_inc(acsf_ready, 1)
            for q in range(3, CONVS):
                conv(0, q)

            heads3 = [P, HPG, HD]

            def by_head(ap):
                return ap.rearrange("p (h d) -> p h d", h=HPG)

            def of_group(t, c, g, n):
                return t[:, bass.ds(HEADS * c + HPG * g, HPG)].unsqueeze(2).to_broadcast([P, HPG, n])

            def y_chunk(g, c):
                return yx[:, bass.ds(GT * g, GT), P * c:P * c + P]

            def tiles(ap):
                return ap.rearrange("p (i t) -> p i t", i=GT)

            def segment(g, c):
                dve.wait_ge(m_landed[c % 2], 16 * (c // 2 + 1) + 32 * g)
                m = by_head(mbuf[:, c % 2, :])
                dve.tensor_tensor(m, m, of_group(acs_t, c, g, P), ALU.subtract).then_inc(seg_step, 1)
                dve.wait_ge(seg_step, 4 * g + c + 1)
                dve.tensor_scalar(m, m, 0.0, None, ALU.min).then_inc(seg_ready, 1)

            def decay_times_cb(g, c):
                dve.wait_ge(exp_done, 4 * g + c + 1)
                m = by_head(mbuf[:, c % 2, :])
                dve.tensor_tensor(m, m, cbm[:, c:c + 1, :].to_broadcast([P, HPG, P]), ALU.mult
                                  ).then_inc(m_ready, 1)

            def add_y(g, c):
                if c == 0:
                    dve.wait_ge(skip_ready, GT * g + GT)
                dve.wait_ge(yd_ready, 4 * g + c + 1)
                y = y_chunk(g, c)
                first = dve.tensor_tensor(y, y, tiles(b_yd[:, :]), ALU.add)
                if c == 0:
                    first.then_inc(y_done, 1)
                    return
                first.then_inc(y_step, 1)
                dve.wait_ge(yo_ready, 3 * g + c)
                dve.wait_ge(e_landed[c % 2], 32 * (c // 2 + 1) + 64 * g if c % 2 else 32 + 32 * g)
                if True:
                    dve.tensor_tensor(tiles(ytmp[:, :]), tiles(b_yo[:, :]), e2[:, c % 2, :, :], ALU.mult
                                      ).then_inc(y_step, 1)
                dve.wait_ge(y_step, 6 * g + 2 * c)
                dve.tensor_tensor(y, y, tiles(ytmp[:, :]), ALU.add).then_inc(y_done, 1)

            def update_state(g, c):
                dve.wait_ge(st_ready, 3 * g + c + 1)
                if c == 0:
                    dve.tensor_copy(state[:, :], b_st[:, :]).then_inc(state_ready, 1)
                    return
                dve.wait_ge(state_ready, 3 * g + c)
                dve.tensor_tensor(by_head(state[:, :]), by_head(state[:, :]), of_group(cd, c, g, HD), ALU.mult
                                  ).then_inc(h_step, 1)
                dve.wait_ge(h_step, 2 * g + c)
                dve.tensor_tensor(state[:, :], state[:, :], b_st[:, :], ALU.add).then_inc(state_ready, 1)

            def token_major(g):
                for c in range(CHUNKS):
                    dve.wait_ge(tok_ready, 6 * g + c + 1)
                    dve.tensor_tensor(by_head(xdt[:, c, :]), by_head(XT_BANK[c][:, :]),
                                      of_group(dt_t[:, :, :].rearrange("p c h -> p (c h)"), c, g, HD), ALU.mult
                                      ).then_inc(xdt_ready, 1)
                dve.wait_ge(tok_ready, 6 * g + 6)
                dve.tensor_tensor(cbm[:, :, :], b_stat[:, :].rearrange("p (c t) -> p c t", c=CHUNKS),
                                  upper.unsqueeze(1).to_broadcast([P, CHUNKS, P]), ALU.mult).then_inc(cbm_ready, 1)

            def norm_y(g, i):
                dve.wait_ge(recip_done, SSM_STAT + g + 1)
                tile = bass.ds(GT * g + i, 1)
                y = yx[:, tile, :]
                dve.scalar_tensor_tensor(out=y, in0=y, scalar=col("norm_g", GT * g + i),
                                         in1=rg[:, :].unsqueeze(1), op0=ALU.mult, op1=ALU.mult
                                         ).then_inc(yn_ready, 1)
                dve.wait_ge(yn_ready, GT * g + i + 1)
                dve.tensor_scalar(act_hi[:, tile, :], y, 1.0, None, ALU.mult).then_inc(yhi_ready, 1)

            def group(g, r, first=False, last=False):
                sched = CHUNK_AFTER_LAST if last else CHUNK_AFTER
                for t in range(PER_GROUP + (2 if last else 0)):
                    if t + 1 in sched:
                        segment(g, sched[t + 1])
                    if t < GT:
                        a = A_SSM + 7 + t
                        dve.wait_ge(wt_used, 2 * (U_GROUP + t + 1) + 2 * r)
                        dve.wait_ge(silu_done, 7 + t - 2 + r)
                        dve.tensor_tensor(tmp[:, (7 + t) % 2, :], acc[a % 2][:, :], rstd[:, :], ALU.mult
                                          ).then_inc(acc_drained, 1)
                    elif last:
                        add_output(t - GT)
                    else:
                        conv(g + 1, t - GT)
                    if t == 0:
                        token_major(g)
                    if not first and t == 2:
                        mean(SSM_STAT - 1 + g, rg, D_INNER // GROUPS)
                    if t in sched:
                        add_y(g, sched[t])
                        if sched[t] < CHUNKS - 1:
                            update_state(g, sched[t])
                    if t + 1 in sched:
                        decay_times_cb(g, sched[t + 1])
                    if not first and t == 2:
                        invert(SSM_STAT - 1 + g, rg, 1 + g)
                    if not first and t in (3, 8 if not last else 6):
                        for i in ((0, 1) if t == 3 else (2, 3)):
                            norm_y(g - 1, i)
                    if t == (7 if last else 9):
                        dve.wait_ge(y_done, 4 * g + 4)
                        y = yx[:, bass.ds(GT * g, GT), :]
                        dve.tensor_tensor(y, y, zs[:, bass.ds(GT * g, GT), :], ALU.mult).then_inc(gated, 1)
                    if last and t == 9:
                        mean(SSM_STAT + g, rg, D_INNER // GROUPS)
                        invert(SSM_STAT + g, rg, 2 + g)
                        for i in range(GT):
                            norm_y(g, i)

            def add_output(n):
                a, m = A_OUT + n, n % KD
                dve.wait_ge(wt_used, 2 * (U_OUT + n + 1))
                dve.tensor_tensor(h[:, m, :], h[:, m, :], acc[a % 2][:, :], ALU.add).then_inc(acc_drained, 1)

            group(0, 0, first=True)
            with dve.Fori(1, GROUPS - 1) as g:
                group(g, PER_GROUP * g)
            group(GROUPS - 1, PER_GROUP * (GROUPS - 1), last=True)
            for m in range(KD):
                add_output(KD + m)
                residue(3, m)

            mlp(U_MLP1, A_MLP1, 32, 6, None)
            mean(7, rstd, D_MODEL)
            invert(7, rstd, 6)
            dve.wait_ge(recip_done, 8)
            for m in range(KD):
                if m % 3 != 2:
                    dve.wait_ge(hg_ready, m + 1)
                    dve.tensor_tensor(hg[:, m, :], hg[:, m, :], rstd[:, :], ALU.mult).then_inc(out_ready, 1)


def kernel(**inputs):
    import numpy as np
    import concourse.bacc as bacc
    from concourse.bass_utils import run_bass_kernel_spmd

    a = {k: np.asarray(v) for k, v in inputs.items()}

    def units(w, k_tiles=8):
        k, n = w.shape
        t = w.reshape(k // (P * k_tiles), k_tiles, P, n // P, P)
        return t.transpose(3, 0, 2, 1, 4).reshape(-1, P, k_tiles * P)

    def mlp(i):
        w1, w2 = a["mlp_w1"][i], a["mlp_w2"][i]
        parts = []
        for blk in range(2):
            cols = slice(blk * BLK * P, (blk + 1) * BLK * P)
            parts += [units(w1[:, cols]), units(w2[cols, :])]
        return parts

    pw = a["pool_w"][0].reshape(2, 2, 2, P, 2, P)
    pool = pw.transpose(0, 3, 1, 4, 2, 5).reshape(2, P, 8 * P)
    w_in = a["ssm_w_in"][0]
    z0, x0, b0, c0 = 0, D_INNER, 2 * D_INNER, 2 * D_INNER + GROUPS * P
    gw = GT * P

    def conv_cols(g):
        return np.r_[b0 - x0 + g * P:b0 - x0 + (g + 1) * P, c0 - x0 + g * P:c0 - x0 + (g + 1) * P,
                     g * gw:(g + 1) * gw]

    ssm = [units(w_in[:, -P:]), units(w_in[:, x0 + conv_cols(0)])]
    for g in range(GROUPS):
        ssm.append(units(w_in[:, z0 + g * gw:z0 + (g + 1) * gw]))
        if g + 1 < GROUPS:
            ssm.append(units(w_in[:, x0 + conv_cols(g + 1)]))
    w_out = a["ssm_w_out"][0]
    out = [units(w_out[:1024]), units(w_out[1024:])]
    weights = np.concatenate([pool, *mlp(0), *ssm, *out, *mlp(1)])
    assert weights.shape[0] == UNITS

    def tiles(v):
        return v.reshape(-1, P).T

    channels = np.concatenate([conv_cols(g) for g in range(GROUPS)])
    rows = lambda v: np.broadcast_to(v, (P, v.shape[-1]))
    table = {
        "g0": tiles(a["norm_mix_g"][0]), "g1": tiles(a["norm_mlp_g"][0]),
        "g2": tiles(a["norm_mix_g"][1]), "g3": tiles(a["norm_mlp_g"][1]), "gf": tiles(a["final_g"]),
        "pool_b": tiles(a["pool_b"][0]), "pool_scale": tiles(a["pool_scale"][0]),
        "conv_w": np.concatenate([tiles(a["ssm_conv_w"][0][k][channels]) for k in range(CONV_K)], axis=1),
        "conv_b": tiles(a["ssm_conv_b"][0][channels]), "norm_g": tiles(a["ssm_norm_g"][0]),
        "skip": tiles(np.repeat(a["ssm_d"][0], HD)),
        "dt_bias": rows(a["ssm_dt_bias"][0]), "a_log": rows(a["ssm_a_log"][0]),
    }
    params = np.concatenate([table[k] for k in COLS], axis=1)
    consts = np.concatenate([np.ones((P, P)), np.triu(np.ones((P, P))), np.eye(P)], axis=1)
    s, l = np.arange(P)[:, None], np.arange(P)[None, :]
    mats = []
    for w in WINDOWS:
        near = (l >= s) & (l - s < w)
        first = near / np.minimum(l + 1, w) - (l == s)
        later = near / w - (l == s)
        before = ((l + P - s < w) / w)[:, :REACH]
        mats.append(np.concatenate([first, before, later, before], axis=1))
    pooling = np.stack(mats, axis=1)
    arrays = {"xt": a["x"][0].T.reshape(KD, P, TOK), "x_tok": a["x"][0].reshape(CHUNKS, P, D_MODEL),
              "pooling": pooling.astype(np.float32), "weights": weights, "params": params,
              "consts": consts.astype(np.float32)}
    arrays = {k: np.ascontiguousarray(v) for k, v in arrays.items()}

    nc = bacc.Bacc("TRN2", target_bir_lowering=False, num_devices=1)
    args = [nc.dram_tensor(k, list(v.shape), F32, kind="ExternalInput").ap() for k, v in arrays.items()]
    out_t = nc.dram_tensor("out_t", [KD, P, TOK], F32, kind="ExternalOutput").ap()
    build(nc, *args, out_t)
    r = run_bass_kernel_spmd(nc, [arrays], core_ids=[0])
    return np.ascontiguousarray(r.results[0]["out_t"].reshape(D_MODEL, TOK).T)[None]
```

```python
from contextlib import ExitStack

import concourse.bass as bass
from concourse import mybir
from concourse.alu_op_type import AluOpType as ALU

F32 = mybir.dt.float32
F32R = mybir.dt.float32r
BF16 = mybir.dt.bfloat16
ACT = mybir.ActivationFunctionType

P = 128
TOK = 512
D_MODEL = 1024
KD = D_MODEL // P
D_FF = 4096
WINDOWS = (2, 4, 8, 16)
REACH = 16
HEADS, HD, GROUPS, CHUNKS, CONV_K = 32, 64, 4, 4, 4
HPG = HEADS // GROUPS
GT = HPG * HD // P
D_INNER = HEADS * HD
CONVS = GT + 2
EPS = 1e-5
N_SOFT = 7

U_POOL = 0
U_MLP0 = 2
BLK = 16
U_SSM = U_MLP0 + 64
U_GROUP = U_SSM + 7
PER_GROUP = GT + CONVS
U_OUT = U_SSM + 1 + 4 * PER_GROUP
U_MLP1 = U_OUT + 16
UNITS = U_MLP1 + 64
A_MLP0 = 2
A_SSM = A_MLP0 + 48
A_OUT = A_SSM + 1 + 4 * PER_GROUP
A_MLP1 = A_OUT + 16
COLS = {}
_at = 0
for _name, _n in (("g0", 8), ("g1", 8), ("g2", 8), ("g3", 8), ("gf", 8), ("pool_b", 8),
                  ("pool_scale", 8), ("conv_w", 96), ("conv_b", 24), ("norm_g", 16), ("skip", 16),
                  ("dt_bias", 32), ("a_log", 32)):
    COLS[_name] = _at
    _at += _n
N_PARAMS = _at
CHUNK_AFTER = {2: 0, 4: 1, 6: 2, 8: 3}
CHUNK_AFTER_LAST = {2: 0, 4: 1, 5: 2, 6: 3}
SEGMENT_AT = {0: 0, 2: 1, 4: 2, 6: 3}
SEGMENT_AT_LAST = {0: 0, 2: 1, 4: 2, 5: 3}
T_GATE, T_SQ, T_STAT = 0, 1, 4
T_NORM, T_NORM_LAST = (6, 8), (6, 7)


def build(nc, xt, x_tok, pooling, weights, params, consts, out_t):
    ctx = ExitStack()
    with ctx:
        sem = lambda name: ctx.enter_context(nc.semaphore(name))
        at = [nc.sbuf_base + 63 & ~63]

        def sb(name, shape, dtype=F32, offset=None):
            size = 4
            for n in shape[1:]:
                size *= n
            where = at[0] if offset is None else offset
            if offset is None:
                at[0] += size + 31 & ~31
            t = nc.alloc_sbuf_tensor_at(name, shape, dtype, offset=where)
            return t, where

        h, _ = sb("residual", [P, KD, TOK])
        xhi, _ = sb("x_hi", [P, KD, TOK], F32R)
        xhi_f = xhi[:, :, :].bitcast(F32)
        xlo, o_xlo = sb("x_lo", [P, KD, TOK], F32R)
        hg, _ = sb("scaled_residual", [P, KD, TOK], F32, o_xlo)
        act_hi, o_hi = sb("act_hi", [P, BLK, TOK], F32R)
        act_hi_f = act_hi[:, :, :].bitcast(F32)
        act_lo, o_lo = sb("act_lo", [P, BLK, TOK], F32R)
        yx, _ = sb("y_accumulated", [P, BLK, TOK], F32, o_lo)
        zs, _ = sb("z_silu", [P, BLK, TOK], F32, o_hi)
        xact, _ = sb("x_conv", [P, GT, TOK], F32, o_hi + 12 * TOK * 4)
        xn, _ = sb("x_token", [P, CHUNKS, D_MODEL], F32, o_hi)
        junk, _ = sb("x_token_squares", [P, D_MODEL], F32, o_lo)
        pools, _ = sb("pooling_matrices", [P, len(WINDOWS), 2 * (P + REACH)], F32, o_lo + 4 * D_MODEL)
        zeros, _ = sb("zeros", [P, TOK], BF16, o_lo + 4 * D_MODEL + 8 * len(WINDOWS) * (P + REACH))
        raw, _ = sb("w_raw", [P, 2, 1024])
        whi, _ = sb("w_hi", [P, 2, 1024], F32R)
        whi_f = whi[:, :, :].bitcast(F32)
        wlo, _ = sb("w_lo", [P, 2, 1024], F32R)
        prm, _ = sb("params", [P, N_PARAMS])
        cst, _ = sb("constants", [P, 3 * P])
        ones, upper, ident = (cst[:, i * P:(i + 1) * P] for i in range(3))
        r_tok, _ = sb("rstd_token", [P, CHUNKS])
        bias, _ = sb("pool_bias", [P, KD])
        tmp, _ = sb("tmp", [P, 2, TOK])
        sq, o_sq = sb("squares", [P, GT, TOK])
        ssq, _ = sb("square_sum", [P, TOK])
        rstd, _ = sb("rstd", [P, TOK])
        pre, _ = sb("conv_in", [P, CONV_K - 1 + TOK])
        bf, _ = sb("b_feature", [P, TOK])
        cf, _ = sb("c_feature", [P, GROUPS, TOK])
        xdt, _ = sb("x_dt", [P, CHUNKS, TOK])
        bt, _ = sb("b_token", [P, CHUNKS, P])
        cbm, _ = sb("cb_masked", [P, CHUNKS, P])
        dec, _ = sb("x_dt_decayed", [P, 2, TOK])
        mbuf, _ = sb("m", [P, 2, HPG * P])
        e2, _ = sb("decay_in", [P, 2, GT, P])
        state, _ = sb("state", [P, TOK])
        ytmp, _ = sb("y_tmp", [P, TOK])
        rg, _ = sb("group_rstd", [P, TOK])
        hd4 = [P, CHUNKS, HEADS]
        dtx, _ = sb("dt_x", hd4)
        neg_abs, _ = sb("dt_neg_abs", hd4)
        ex, _ = sb("dt_exp", hd4)
        mx, _ = sb("dt_max", hd4)
        rc, _ = sb("dt_rc", hd4)
        ser, _ = sb("dt_series", hd4)
        s2, _ = sb("dt_s2", hd4)
        dt_t, _ = sb("dt_token", hd4)
        adt, _ = sb("a_dt", hd4)
        exp_a, _ = sb("exp_a", [P, HEADS])
        cum, _ = sb("cumulated", [P, 2, CHUNKS * HEADS])
        acs_t = cum[:, 0, :]
        dend, _ = sb("decay_to_end", [P, CHUNKS * HEADS])
        cd, _ = sb("chunk_decay", [P, CHUNKS * HEADS])
        diag = sq[:, GT - 1, :]
        acs_f, _ = sb("a_cs_feature", [HEADS, TOK], F32, o_sq)
        eacs_f, _ = sb("exp_a_cs_feature", [HEADS, TOK], F32, o_sq + TOK * 4)
        assert at[0] <= nc.sbuf_usable_end, (at[0], nc.sbuf_usable_end)

        acs_dram = nc.dram_tensor("acs_scratch", [GROUPS, CHUNKS, HPG, P], F32).ap()
        eacs_dram = nc.dram_tensor("eacs_scratch", [GROUPS, CHUNKS, HPG, P], F32).ap()

        bank = [ctx.enter_context(nc.psum_tensor(f"bank{i}", [P, TOK], F32)) for i in range(8)]
        acc = bank[0:2]
        XT_BANK = (bank[2], bank[4], bank[5], bank[6])
        b_misc, b_yd, b_yo, b_st, b_stat = bank[3], bank[4], bank[5], bank[6], bank[7]

        x_landed = [sem(f"x_landed{m}") for m in range(KD)]
        xtok_landed = [sem(f"x_token_landed{c}") for c in range(CHUNKS)]
        pools_landed = sem("pooling_matrices_landed")
        sum_ready = sem("x_sums_ready")
        tok_mean = sem("x_mean_ready")
        tok_root = sem("x_root_ready")
        xn_ready = sem("x_token_normed")
        zeros_ready = sem("zeros_ready")
        mix_ready = sem("mix_ready")
        bias_ready = sem("pool_bias_ready")
        biased = sem("x_biased")
        biased_pool = sem("x_biased_pool")
        params_landed = sem("params_landed")
        consts_landed = sem("consts_landed")
        raw_landed = [sem("raw_landed0"), sem("raw_landed1")]
        hi_ready = sem("w_hi_ready")
        lo_ready = sem("w_lo_ready")
        wt_used = sem("w_used")
        acc_drained = sem("acc_drained")
        pool_added = sem("pool_added")
        h_done = sem("h_done")
        pooled_hi = sem("pooled_hi_ready")
        pooled_lo = sem("pooled_lo_ready")
        xhi_ready = sem("x_hi_ready")
        xlo_ready = sem("x_lo_ready")
        sq_ready = sem("sq_ready")
        ssq_added = sem("ssq_added")
        stat_ready = sem("stat_ready")
        stat_drained = sem("stat_drained")
        sqrt_done = sem("sqrt_done")
        inverted = sem("token_rstd_ready")
        recip_done = sem("recip_done")
        diag_ready = sem("rstd_diagonal_ready")
        spread_ready = sem("rstd_spread")
        pads_clear = sem("pads_clear")
        chain = sem("dve_chain")
        hid_sq_ready = sem("hidden_square_ready")
        hid_hi_ready = sem("hidden_hi_ready")
        hid_lo_ready = sem("hidden_lo_ready")
        conv_step = sem("conv_step")
        conv_ready = sem("conv_ready")
        silu_done = sem("silu_done")
        skip_ready = sem("skip_ready")
        dtt_ready = sem("dt_transposed")
        dt_na = sem("dt_neg_abs_ready")
        dt_exp = sem("dt_exp_ready")
        adt_ready = sem("adt_ready")
        cum_ready = sem("cum_ready")
        acsf_ready = sem("acs_f_ready")
        dend_in = sem("decay_exponent_ready")
        decays = sem("decays_ready")
        scratch = sem("scratch_written")
        tok_ready = sem("token_major_ready")
        xdt_ready = sem("x_dt_ready")
        cbm_ready = sem("cb_ready")
        bt_ready = sem("b_token_ready")
        dec_ready = sem("dec_ready")
        m_landed = [sem("m_landed0"), sem("m_landed1")]
        e_landed = [sem("e_landed0"), sem("e_landed1")]
        seg_step = sem("segment_step")
        seg_ready = sem("segment_ready")
        exp_done = sem("exp_done")
        m_ready = sem("m_ready")
        yd_ready = sem("y_diag_ready")
        yo_ready = sem("y_off_ready")
        st_ready = sem("state_ready")
        y_step = sem("y_step")
        y_done = sem("y_done")
        h_step = sem("state_step")
        state_ready = sem("state_updated")
        gated = sem("gated")
        yn_ready = sem("y_normed")
        yhi_ready = sem("y_hi_ready")
        ylo_ready = sem("y_lo_ready")
        hg_ready = sem("scaled_ready")
        out_ready = sem("out_ready")
        out_written = sem("out_written")

        def col(name, i, n=1):
            return prm[:, bass.ds(COLS[name] + i, n)]

        prep_from = [None, None, (h_done, 8), (acc_drained, A_OUT + 8), (h_done, 24)]
        gains = ["g0", "g1", "g2", "g3", "gf"]
        sq_base = [None, 0, 8, 32, 40]
        add_base = [None, 1, 10, 31, 40]
        stat_of = [None, 0, 1, 6, 7]
        SSM_SQ, SSM_ADD, SSM_STAT = 16, 18, 2

        block = ctx.enter_context(nc.Block())

        @block.sync
        def _(sp):
            def load_weights(c, r=0):
                if c >= 2:
                    sp.wait_ge(lo_ready, 2 * (c - 1) + 2 * r)
                sp.dma_start(raw[:, c % 2, :], weights[bass.ds(c + r, 1), :, :].rearrange("a p n -> (a p) n")
                             ).then_inc(raw_landed[c % 2], 16)

            def load_acs(g, c):
                sp.dma_start(mbuf[:, c % 2, :],
                             acs_dram[bass.ds(g, 1), c, :, :].rearrange("g h t -> g (h t)")
                             .to_broadcast([P, HPG * P])).then_inc(m_landed[c % 2], 16)

            def load_exp_acs(g, c):
                heads = eacs_dram[bass.ds(g, 1), c, :, :].rearrange("g (i two) t -> g two i t", two=2)
                for half in range(2):
                    sp.dma_start(e2[64 * half:64 * half + 64, c % 2, :, :],
                                 heads[:, half, :, :].to_broadcast([64, GT, P])).then_inc(e_landed[c % 2], 16)

            for c in range(CHUNKS):
                sp.dma_start(xn[:, c, :], x_tok[c, :, :]).then_inc(xtok_landed[c], 16)
            load_weights(0)
            for m in range(KD):
                if m == 2:
                    load_weights(1)
                sp.dma_start(h[:, m, :], xt[m, :, :]).then_inc(x_landed[m], 16)
            sp.dma_start(cst[:, :], consts).then_inc(consts_landed, 16)
            with sp.Fori(0, (U_GROUP - 1) // 2 - 1) as i:
                load_weights(2, 2 * i)
                load_weights(3, 2 * i)
            load_weights(U_GROUP - 1)
            load_weights(U_GROUP)
            sp.wait_ge(acsf_ready, 1)
            sp.wait_ge(decays, 3)
            for g in range(GROUPS):
                for src, dst in ((acs_f, acs_dram), (eacs_f, eacs_dram)):
                    sp.dma_start(dst[g].rearrange("c h t -> h c t"),
                                 src[g * HPG:(g + 1) * HPG, :].rearrange("h (c t) -> h c t", c=CHUNKS)
                                 ).then_inc(scratch, 16)
            load_weights(U_GROUP + 1)
            load_weights(U_GROUP + 2)
            sp.wait_ge(scratch, 2 * GROUPS * 16)
            load_acs(0, 0)

            def group_loads(g, r, first=False, last=False):
                after = {c: t for t, c in (CHUNK_AFTER_LAST if last else CHUNK_AFTER).items()}
                for t in range(PER_GROUP):
                    load_weights(U_GROUP + 3 + t, r)
                    if t == 0:
                        if not first:
                            sp.wait_ge(yd_ready, 4 * g)
                        load_acs(g, 1)
                    if t == 1:
                        if not first:
                            sp.wait_ge(y_done, 4 * g)
                        load_exp_acs(g, 1)
                        load_exp_acs(g, 2)
                    for c in (2, 3):
                        if t == after[c - 2] + 1:
                            sp.wait_ge(yd_ready, 4 * g + c - 1)
                            load_acs(g, c)
                    if t == after[1] + 2:
                        sp.wait_ge(y_done, 4 * g + 2)
                        load_exp_acs(g, 3)
                    if not last and t == after[2] + 1:
                        sp.wait_ge(yd_ready, 4 * g + 3)
                        load_acs(g + 1, 0)

            group_loads(0, 0, first=True)
            with sp.Fori(1, GROUPS - 1) as g:
                group_loads(g, PER_GROUP * g)
            group_loads(GROUPS - 1, PER_GROUP * (GROUPS - 1), last=True)
            rest = U_GROUP + 3 + 4 * PER_GROUP
            with sp.Fori(0, (UNITS - rest) // 2) as i:
                load_weights(rest, 2 * i)
                load_weights(rest + 1, 2 * i)
            for u in range(rest + (UNITS - rest) // 2 * 2, UNITS):
                load_weights(u)
            for m in range(KD):
                sp.wait_ge(out_ready, m + 1)
                sp.dma_start(out_t[m, :, :], hg[:, m, :]).then_inc(out_written, 16)
            sp.wait_ge(out_written, 16 * KD)

        @block.scalar
        def _(act):
            act.dma_start(pools[:, :, :], pooling).then_inc(pools_landed, 16)
            act.dma_start(prm[:, :], params).then_inc(params_landed, 16)

            def round_half(c, half, r=0):
                if isinstance(r, int) and c + r >= UNITS:
                    return
                if half == 0:
                    act.wait_ge(raw_landed[c % 2], 16 * (c // 2 + 1) + 8 * r)
                if c >= 2:
                    act.wait_ge(wt_used, 2 * (c - 2) + half + 1 + 2 * r)
                part = slice(512 * half, 512 * half + 512)
                act.activation(whi[:, c % 2, part], raw[:, c % 2, part], ACT.Copy).then_inc(hi_ready, 1)

            def round_weights(c, r=0):
                round_half(c, 0, r)
                round_half(c, 1, r)

            def square(m, slot):
                act.activation(sq[:, slot, :], h[:, bass.ds(m, 1), :].rearrange("p a t -> p (a t)"),
                               ACT.Square).then_inc(sq_ready, 1)

            def prepare(n, m, slot, last=False):
                if slot is not None:
                    act.wait_ge(ssq_added, add_base[n] + m - 1)
                s, count = prep_from[n] if n > 1 else (acc_drained, 0) if m < 2 else (pool_added, -2)
                act.wait_ge(s, count + m + 1)
                if last and isinstance(m, int) and m == KD - 1:
                    square(m, slot)
                if last:
                    act.activation(hg[:, bass.ds(m, 1), :], h[:, bass.ds(m, 1), :], ACT.Copy,
                                   scale=col(gains[n], m)).then_inc(hg_ready, 1)
                else:
                    act.activation(xhi[:, bass.ds(m, 1), :], h[:, bass.ds(m, 1), :], ACT.Copy,
                                   scale=col(gains[n], m)).then_inc(xhi_ready, 1)
                if slot is not None and not (last and isinstance(m, int) and m == KD - 1):
                    square(m, slot)

            def root(k, buf=r_tok):
                act.wait_ge(stat_drained, k + 1)
                act.activation(buf[:, :], buf[:, :], ACT.Sqrt).then_inc(sqrt_done, 1)

            act.wait_ge(ssq_added, 1)
            act.activation(tmp[:, 0, 0:1], ssq[:, 0:1], ACT.Sqrt)
            for c in range(CHUNKS):
                act.wait_ge(xtok_landed[c], 16)
                act.activation(junk[:, :], xn[:, c, :], ACT.Square, accum_out=r_tok[:, c:c + 1]
                               ).then_inc(sum_ready, 1)
                act.wait_ge(tok_mean, c + 1)
                act.activation(r_tok[:, c:c + 1], r_tok[:, c:c + 1], ACT.Sqrt).then_inc(tok_root, 1)
            act.wait_ge(params_landed, 16)

            def pooled(m):
                act.wait_ge(mix_ready, m + 1)
                act.activation(xhi[:, m, :], bank[m][:, :], ACT.Copy, scale=col("g0", m)
                               ).then_inc(pooled_hi, 1)

            def add_bias(m):
                act.wait_ge(x_landed[m], 16)
                act.activation(h[:, m, :], h[:, m, :], ACT.Identity, bias=bias[:, m:m + 1]).then_inc(biased, 1)

            round_weights(0)
            for m in range(6):
                pooled(m)
            act.wait_ge(bias_ready, 1)
            add_bias(0)
            add_bias(1)
            round_weights(1)
            pooled(6)
            pooled(7)
            for m in range(2, 5):
                add_bias(m)
            prepare(1, 0, None)
            prepare(1, 1, None)
            round_half(2, 0)
            prepare(1, 2, None)
            prepare(1, 3, None)
            round_half(2, 1)
            for m in range(4, KD):
                prepare(1, m, None)
            round_weights(3)

            def mlp(u0, blk_base, n, n_next):
                for blk in range(2):
                    hid = blk_base + 16 * blk
                    with act.Fori(0, BLK // 2) as i:
                        for e in range(2):
                            round_weights(u0 + 32 * blk + e + 2, 2 * i)
                            if blk == 0 and e == 0:
                                act.wait_ge(ssq_added, add_base[n] + i)
                                square(i, 0)
                            act.wait_ge(hid_sq_ready, hid + e + 1 + 2 * i)
                            act.activation(act_hi[:, bass.ds(2 * i + e, 1), :], tmp[:, e:e + 1, :],
                                           ACT.Copy).then_inc(hid_hi_ready, 1)

                    def down(i, r):
                        for e in range(4):
                            round_weights(u0 + 32 * blk + BLK + e + 2, r)
                            if blk == 1 and e % 2:
                                prepare(n_next, 2 * i + e // 2, e // 2, n_next == 4)

                    with act.Fori(0, 3) as i:
                        down(i, 4 * i)
                    down(3, 12)

            mlp(U_MLP0, 0, 1, 2)

            def silu(dst, slot):
                act.activation(dst, tmp[:, slot:slot + 1, :], ACT.Silu).then_inc(silu_done, 1)

            def conv_silu(g, q):
                act.wait_ge(conv_ready, CONVS * g + q + 1)
                dst = (bf[:, :].unsqueeze(1) if q == 0 else cf[:, bass.ds(g, 1), :] if q == 1
                       else xact[:, q - 2:q - 1, :])
                silu(dst, (q + 1) % 2)
                if q >= 2:
                    act.wait_ge(silu_done, PER_GROUP * g + q + 1)
                    act.activation(yx[:, bass.ds(GT * g + q - 2, 1), :], xact[:, q - 2:q - 1, :], ACT.Copy,
                                   scale=col("skip", GT * g + q - 2)).then_inc(skip_ready, 1)

            round_weights(U_SSM + 2)
            root(1, rstd)
            act.activation(exp_a[:, :], col("a_log", 0, HEADS), ACT.Exp).then_inc(dt_exp, 1)
            round_weights(U_SSM + 3)
            act.wait_ge(dt_na, 1)
            act.activation(ex[:, :, :], neg_abs[:, :, :], ACT.Exp).then_inc(dt_exp, 1)
            for j in range(2, 7):
                round_half(U_SSM + 2 + j, 0)
                conv_silu(0, j - 2)
                round_half(U_SSM + 2 + j, 1)
                if j == 4:
                    act.wait_ge(dend_in, 1)
                    act.activation(dend[:, :], dend[:, :], ACT.Exp).then_inc(decays, 1)
                    act.activation(cd[:, :], cum[:, 1, :], ACT.Exp).then_inc(decays, 1)
                    act.wait_ge(acsf_ready, 1)
                    act.activation(eacs_f[:, :], acs_f[:, :], ACT.Exp).then_inc(decays, 1)

            def exp_segments(g, c):
                act.wait_ge(seg_ready, 4 * g + c + 1)
                act.activation(mbuf[:, c % 2, :], mbuf[:, c % 2, :], ACT.Exp).then_inc(exp_done, 1)

            def group_squares(g):
                act.wait_ge(gated, g + 1)
                for i in range(GT):
                    act.activation(sq[:, i:i + 1, :], yx[:, bass.ds(GT * g + i, 1), :],
                                   ACT.Square).then_inc(sq_ready, 1)

            def group(g, r, first=False, last=False):
                sched = CHUNK_AFTER_LAST if last else CHUNK_AFTER
                segs = SEGMENT_AT_LAST if last else SEGMENT_AT
                for t in range(PER_GROUP + (2 if last else 0)):
                    round_half(U_GROUP + t + 2, 0, r)
                    if t == 0:
                        conv_silu(g, CONVS - 1)
                    elif t <= GT:
                        z = t - 1
                        act.wait_ge(acc_drained, A_SSM + 8 + z + r)
                        if z == 0 and last:
                            act.wait_ge(tok_ready, 6 * g + CHUNKS)
                        silu(zs[:, bass.ds(GT * g + z, 1), :], (z + 1) % 2)
                    elif not last:
                        conv_silu(g + 1, t - GT - 1)
                    if last and t == 7:
                        group_squares(g)
                    round_half(U_GROUP + t + 2, 1, r)
                    if t == 0:
                        act.wait_ge(tok_ready, 6 * g + CHUNKS + 1)
                        act.activation(bt[:, :, :], b_misc[:, :].rearrange("p (c n) -> p c n", c=CHUNKS),
                                       ACT.Copy).then_inc(bt_ready, 1)
                    if not first and t == T_SQ:
                        group_squares(g - 1)
                    if t in segs:
                        exp_segments(g, segs[t])
                    if not first and t == T_STAT:
                        root(SSM_STAT - 1 + g)
                    if last and t == 9:
                        root(SSM_STAT + g)

            group(0, 0, first=True)
            with act.Fori(1, GROUPS - 1) as g:
                group(g, PER_GROUP * g)
            group(GROUPS - 1, PER_GROUP * (GROUPS - 1), last=True)
            for m in range(KD):
                round_weights(U_OUT + 8 + m + 2)
                prepare(3, m, None)

            mlp(U_MLP1, 32, 3, 4)
            root(7)

        @block.gpsimd
        def _(pool):
            pool.memset(pre[:, 0:CONV_K - 1], 0.0).then_inc(pads_clear, 1)

            def split_half(c, half, r=0):
                if isinstance(r, int) and c + r >= UNITS:
                    return
                pool.wait_ge(hi_ready, 2 * c + half + 1 + 2 * r)
                part = slice(512 * half, 512 * half + 512)
                pool.tensor_tensor(wlo[:, c % 2, part], raw[:, c % 2, part], whi_f[:, c % 2, part],
                                   ALU.subtract).then_inc(lo_ready, 1)

            def split_weights(c, r=0):
                split_half(c, 0, r)
                split_half(c, 1, r)

            def clear_sum(n):
                if n > 1:
                    pool.wait_ge(stat_ready, stat_of[n])
                pool.memset(ssq[:, :], 0.0).then_inc(ssq_added, 1)

            def add_squares(n, m, slot):
                pool.wait_ge(sq_ready, sq_base[n] + m + 1)
                pool.wait_ge(ssq_added, add_base[n] + m)
                pool.tensor_tensor(ssq[:, :], ssq[:, :], sq[:, slot, :], ALU.add).then_inc(ssq_added, 1)

            clear_sum(1)

            split_weights(0)
            split_weights(1)
            pool.wait_ge(bias_ready, 1)
            for m in range(5, KD):
                pool.wait_ge(x_landed[m], 16)
                pool.tensor_tensor(h[:, m, :], h[:, m, :], bias[:, m:m + 1].to_broadcast([P, TOK]), ALU.add
                                   ).then_inc(biased_pool, 1)
            split_weights(2)
            split_weights(3)

            def mlp(u0, n, n_next):
                for blk in range(2):
                    with pool.Fori(0, BLK // 2) as i:
                        split_weights(u0 + 32 * blk + 2, 2 * i)
                        if blk == 0:
                            add_squares(n, i, 0)
                        split_weights(u0 + 32 * blk + 3, 2 * i)
                    if blk == 1:
                        clear_sum(n_next)

                    def down(i, r):
                        for e in range(4):
                            split_weights(u0 + 32 * blk + BLK + e + 2, r)
                            if n_next == 4 and isinstance(i, int) and e == 3:
                                continue
                            if blk == 1 and e % 2:
                                add_squares(n_next, 2 * i + e // 2, e // 2)

                    with pool.Fori(0, 3) as i:
                        down(i, 4 * i)
                    down(3, 12)

            mlp(U_MLP0, 1, 2)
            for j in range(7):
                split_weights(U_SSM + 2 + j)

            def decayed(g, c):
                pool.wait_ge(xdt_ready, 4 * g + c + 1)
                if c == 2:
                    pool.wait_ge(st_ready, 3 * g + 1)
                pool.tensor_tensor(
                    dec[:, c % 2, :].rearrange("p (h d) -> p h d", h=HPG),
                    xdt[:, c, :].rearrange("p (h d) -> p h d", h=HPG),
                    dend[:, bass.ds(HEADS * c + HPG * g, HPG)].unsqueeze(2).to_broadcast([P, HPG, HD]),
                    ALU.mult).then_inc(dec_ready, 1)

            def group_sum(g, of=(1, 2, 3)):
                if of[0] == 1:
                    pool.wait_ge(stat_ready, SSM_STAT + g)
                for i in of:
                    pool.wait_ge(sq_ready, SSM_SQ + GT * g + i + 1)
                    if i > 1:
                        pool.wait_ge(ssq_added, SSM_ADD + (GT - 1) * g + i - 1)
                    pool.tensor_tensor(ssq[:, :], sq[:, 0, :] if i == 1 else ssq[:, :], sq[:, i, :],
                                       ALU.add).then_inc(ssq_added, 1)

            def y_residue(g, i):
                pool.wait_ge(yhi_ready, GT * g + i + 1)
                tile = bass.ds(GT * g + i, 1)
                pool.tensor_tensor(act_lo[:, tile, :], yx[:, tile, :], act_hi_f[:, tile, :],
                                   ALU.subtract).then_inc(ylo_ready, 1)

            def group(g, r, first=False, last=False):
                t_norm = T_NORM_LAST if last else T_NORM
                for t in range(PER_GROUP + (2 if last else 0)):
                    split_half(U_GROUP + 2 + t, 0, r)
                    if t == 1:
                        pool.wait_ge(decays, 1)
                        decayed(g, 0)
                        decayed(g, 1)
                    if t == 3:
                        decayed(g, 2)
                    if not first and t == T_SQ + 2:
                        group_sum(g - 1, (3,))
                    if not first and t == t_norm[0] + 1:
                        y_residue(g - 1, 0)
                        y_residue(g - 1, 1)
                    split_half(U_GROUP + 2 + t, 1, r)
                    if not first and t == T_SQ + 1:
                        group_sum(g - 1, (1, 2))
                    if not first and t == t_norm[1] + 1:
                        y_residue(g - 1, 2)
                        y_residue(g - 1, 3)
                    if last and t == 7:
                        group_sum(g)
                    if last and t in (9, 10):
                        y_residue(g, 2 * (t - 9))
                        y_residue(g, 2 * (t - 9) + 1)

            group(0, 0, first=True)
            with pool.Fori(1, GROUPS - 1) as g:
                group(g, PER_GROUP * g)
            group(GROUPS - 1, PER_GROUP * (GROUPS - 1), last=True)
            clear_sum(3)
            for m in range(KD):
                split_weights(U_OUT + 8 + m + 2)
            mlp(U_MLP1, 3, 4)

        @block.tensor
        def _(pe):
            def three(out, wh, wl, xh, xl, start, stop):
                pe.matmul(out, wh, xh, start=start, stop=False)
                pe.matmul(out, wh, xl, start=False, stop=False)
                return pe.matmul(out, wl, xh, start=False, stop=stop)

            def unit(c, r, out, hi, lo, tile0, start=True, stop=True, tile_wait=None, between=None):
                for k in range(8):
                    if k == 4 and between is not None:
                        between()
                    if k % 4 == 0:
                        pe.wait_ge(lo_ready, 2 * c + k // 4 + 1 + 2 * r)
                    if tile_wait is not None:
                        tile_wait(k)
                    w = slice(P * k, P * k + P)
                    last = three(out, whi[:, c % 2, w], wlo[:, c % 2, w], hi[:, tile0 + k, :],
                                 lo[:, tile0 + k, :], start and k == 0, stop and k == 7)
                    if k % 4 == 3:
                        last.then_inc(wt_used, 1)

            def accumulator(a, r=0):
                pe.wait_ge(acc_drained, a - 1 + r)
                return acc[a % 2][:, :]

            def statistic(tiles):
                pe.wait_ge(ssq_added, tiles)
                pe.matmul(b_stat[:, :], ones, ssq[:, :], start=True, stop=True).then_inc(stat_ready, 1)

            def statistic_by_token(tiles):
                pe.wait_ge(ssq_added, tiles)
                for c in range(CHUNKS):
                    last = pe.matmul(b_stat[:, c:c + 1], ssq[:, P * c:P * c + P], ones[:, 0:1],
                                     start=True, stop=True)
                last.then_inc(stat_ready, 1)

            def spread(n):
                pe.wait_ge(diag_ready, CHUNKS * (n + 1))
                pe.matmul(b_stat[:, :], ones, diag[:, :], start=True, stop=True).then_inc(spread_ready, 1)

            pe.wait_ge(zeros_ready, 1)
            for m in range(2 * KD):
                pe.matmul(bank[m % KD][:, :], zeros[:, 0:P], zeros[:, :], start=m < KD, stop=False)
            pe.wait_ge(pools_landed, 16)
            for c in range(CHUNKS):
                n = P if c == CHUNKS - 1 else P + REACH
                for m in range(KD):
                    if m % 4 == 0:
                        pe.wait_ge(xn_ready, 2 * c + m // 4 + 1)
                    o = 0 if c == 0 else P + REACH
                    last = pe.matmul(bank[m][:, P * c:P * c + n], xn[:, c, P * m:P * m + P],
                                     pools[:, m // 2, o:o + n], start=False, stop=c == CHUNKS - 1)
                    if c == CHUNKS - 1:
                        last.then_inc(mix_ready, 1)

            def pool_maps(gi):
                pe.wait_ge(lo_ready, gi + 1)
                pe.wait_ge(pooled_lo, 2 * gi + 2)
                for mt in range(2):
                    for k in range(2):
                        w = bass.ds(512 * (gi % 2) + 256 * mt + 128 * k, P)
                        last = three(bank[2 * gi + mt][:, :], whi[:, gi // 2, w], wlo[:, gi // 2, w],
                                     xhi[:, 2 * gi + k, :], xlo[:, 2 * gi + k, :], k == 0, k == 1)
                last.then_inc(wt_used, 1)

            for gi in range(4):
                pool_maps(gi)

            def mlp(u0, a0, x_base, hid_base, squares):
                for blk in range(2):
                    with pe.Fori(0, BLK // 2) as i:
                        for e in range(2):
                            out = accumulator(a0 + 24 * blk + e, 2 * i)
                            unit(u0 + 32 * blk + e, 2 * i, out, xhi, xlo, 0,
                                 tile_wait=(lambda k: pe.wait_ge(xlo_ready, x_base + k + 1)) if e == 0 else None)
                    if blk == 0:
                        statistic(squares)
                    base = hid_base + BLK * blk
                    with pe.Fori(0, KD // 2) as i:
                        for e in range(2):
                            out = accumulator(a0 + 24 * blk + BLK + e, 2 * i)
                            for half in range(2):
                                unit(u0 + 32 * blk + BLK + 2 * e + half, 4 * i, out, act_hi, act_lo, 8 * half,
                                     start=half == 0, stop=half == 1,
                                     tile_wait=(lambda k, f=half: pe.wait_ge(hid_lo_ready, base + 8 * f + k + 1))
                                     if e == 0 else None)

            pe.wait_ge(consts_landed, 16)
            mlp(U_MLP0, A_MLP0, 0, 0, 9)

            unit(U_SSM, 0, accumulator(A_SSM), xhi, xlo, 0,
                 tile_wait=lambda k: pe.wait_ge(xlo_ready, 8 + k + 1))
            statistic(SSM_ADD)
            unit(U_SSM + 1, 0, accumulator(A_SSM + 1), xhi, xlo, 0)
            pe.wait_ge(acc_drained, A_SSM + 1)
            for c in range(CHUNKS):
                last = pe.transpose(b_misc[:, P * c:P * c + P], tmp[:, 0, P * c:P * c + P], ident)
            last.then_inc(dtt_ready, 1)
            for j in (2, 3):
                unit(U_SSM + j, 0, accumulator(A_SSM + j), xhi, xlo, 0)
            pe.wait_ge(adt_ready, 1)
            flat = adt[:, :, :].rearrange("p c h -> p (c h)")
            pe.matmul(b_stat[:, 0:P], upper, flat, start=True, stop=True)
            pe.matmul(b_stat[:, P:2 * P], ones, flat, start=True, stop=True)
            for c in range(CHUNKS):
                last = pe.matmul(bank[2][0:HEADS, P * c:P * c + P], adt[:, c, :], upper, start=True, stop=True)
            last.then_inc(cum_ready, 1)
            for j in range(4, 7):
                unit(U_SSM + j, 0, accumulator(A_SSM + j), xhi, xlo, 0)

            def token_major(g, first):
                pe.wait_ge(silu_done, PER_GROUP * g + CONVS)
                pe.wait_ge(recip_done, SSM_STAT + g - (0 if first else 1))
                if not first:
                    pe.wait_ge(y_step, 6 * g)
                for c in range(CHUNKS):
                    for i in range(GT):
                        last = pe.transpose(XT_BANK[c][:, P * i:P * i + P], xact[:, i, P * c:P * c + P], ident)
                    last.then_inc(tok_ready, 1)
                for c in range(CHUNKS):
                    last = pe.transpose(b_misc[:, P * c:P * c + P], bf[:, P * c:P * c + P], ident)
                last.then_inc(tok_ready, 1)
                for c in range(CHUNKS):
                    last = pe.matmul(b_stat[:, P * c:P * c + P], bf[:, P * c:P * c + P],
                                     c_chunk(g, c), start=True, stop=True)
                last.then_inc(tok_ready, 1)

            def c_chunk(g, c):
                return cf[:, bass.ds(g, 1), P * c:P * c + P].rearrange("p a t -> p (a t)")

            def chunk(g, c):
                pe.wait_ge(m_ready, 4 * g + c + 1)
                if c:
                    pe.wait_ge(y_done, 4 * g + c)
                for hh in range(HPG):
                    last = pe.matmul(b_yd[64 * (hh % 2):64 * (hh % 2) + 64, P * (hh // 2):P * (hh // 2) + P],
                                     xdt[:, c, HD * hh:HD * hh + HD], mbuf[:, c % 2, P * hh:P * hh + P],
                                     start=True, stop=True)
                last.then_inc(yd_ready, 1)
                if c:
                    pe.wait_ge(state_ready, 3 * g + c)
                    for i in range(GT):
                        last = pe.matmul(b_yo[:, P * i:P * i + P], state[:, P * i:P * i + P], c_chunk(g, c),
                                         start=True, stop=True)
                    last.then_inc(yo_ready, 1)
                if c < CHUNKS - 1:
                    pe.wait_ge(dec_ready, 3 * g + c + 1)
                    pe.wait_ge(bt_ready, g + 1)
                    pe.matmul(b_st[:, :], bt[:, c, :], dec[:, c % 2, :], start=True, stop=True).then_inc(st_ready, 1)

            def group(g, r, first=False, last=False):
                sched = CHUNK_AFTER_LAST if last else CHUNK_AFTER
                segs = SEGMENT_AT_LAST if last else SEGMENT_AT
                for t in range(PER_GROUP + (2 if last else 0)):
                    if last and t >= GT:
                        unit(U_OUT + t - GT, 0, accumulator(A_OUT + t - GT), act_hi, act_lo, 0,
                             tile_wait=(lambda k: pe.wait_ge(ylo_ready, k + 1)) if t == GT else None,
                             between=(lambda: spread(g)) if t == PER_GROUP else None)
                    else:
                        unit(U_GROUP + t, r, accumulator(A_SSM + 7 + t, r), xhi, xlo, 0)
                    if t == 0:
                        token_major(g, first)
                    if not first and t == T_STAT:
                        pe.wait_ge(cbm_ready, g + 1)
                        statistic_by_token(SSM_ADD + (GT - 1) * g)
                    if not first and t == T_STAT + 1:
                        spread(g - 1)
                    if t in sched:
                        chunk(g, sched[t])
                    if last and t == 9:
                        statistic_by_token(SSM_ADD + (GT - 1) * (g + 1))

            group(0, 0, first=True)
            with pe.Fori(1, GROUPS - 1) as g:
                group(g, PER_GROUP * g)
            group(GROUPS - 1, PER_GROUP * (GROUPS - 1), last=True)
            for m in range(KD):
                unit(U_OUT + KD + m, 0, accumulator(A_OUT + KD + m), act_hi, act_lo, 8,
                     tile_wait=(lambda k: pe.wait_ge(ylo_ready, 8 + k + 1)) if m == 0 else None)

            mlp(U_MLP1, A_MLP1, 16, 32, 39)
            pe.wait_ge(ssq_added, add_base[4] + KD - 1)
            for c in range(CHUNKS):
                pe.matmul(bank[2 + c][:, 0:1], ssq[:, P * c:P * c + P], ones[:, 0:1], start=True, stop=False)
            pe.wait_ge(sq_ready, sq_base[4] + KD)
            for c in range(CHUNKS):
                last = pe.matmul(bank[2 + c][:, 0:1], sq[:, 1, P * c:P * c + P], ones[:, 0:1],
                                 start=False, stop=True)
            last.then_inc(stat_ready, 1)
            for c in range(CHUNKS):
                pe.wait_ge(diag_ready, CHUNKS * GROUPS + c + 1)
                last = pe.matmul(b_stat[:, P * c:P * c + P], ones, diag[:, P * c:P * c + P], start=True, stop=True)
            last.then_inc(spread_ready, 1)

        @block.vector
        def _(dve):
            steps = [0]

            def link(ins):
                steps[0] += 1
                ins.then_inc(chain, 1)
                dve.wait_ge(chain, steps[0])

            def residue(n, m):
                dve.wait_ge(xhi_ready, 8 * (n - 1) + m + 1)
                tile = bass.ds(m, 1)
                dve.scalar_tensor_tensor(out=xlo[:, tile, :], in0=h[:, tile, :], scalar=col(gains[n], m),
                                         in1=xhi_f[:, tile, :], op0=ALU.mult, op1=ALU.subtract
                                         ).then_inc(xlo_ready, 1)

            def mean(k, buf, n):
                dve.wait_ge(stat_ready, k + 1)
                dve.tensor_scalar(buf[:, :], b_stat[:, :], 1.0 / n, EPS, ALU.mult, ALU.add
                                  ).then_inc(stat_drained, 1)

            def invert(k, buf, roots):
                if roots is None:
                    dve.wait_ge(stat_drained, k + 1)
                else:
                    dve.wait_ge(sqrt_done, roots)
                dve.reciprocal(buf[:, :], buf[:, :]).then_inc(recip_done, 1)

            def diagonals(k, n, roots):
                dve.wait_ge(stat_ready, k + 1)
                dve.tensor_scalar(r_tok[:, :], b_stat[:, 0:CHUNKS], 1.0 / n, EPS, ALU.mult, ALU.add
                                  ).then_inc(stat_drained, 1)
                make_diagonals(roots)

            def make_diagonals(roots):
                dve.wait_ge(sqrt_done, roots)
                dve.reciprocal(r_tok[:, :], r_tok[:, :]).then_inc(inverted, 1)
                dve.wait_ge(inverted, roots - 1)
                for c in range(CHUNKS):
                    dve.tensor_scalar(diag[:, P * c:P * c + P], ident, r_tok[:, c:c + 1], None, ALU.mult
                                      ).then_inc(diag_ready, 1)

            dve.memset(zeros[:, :], 0.0).then_inc(zeros_ready, 1)
            for c in range(CHUNKS):
                r = r_tok[:, c:c + 1]
                dve.wait_ge(sum_ready, c + 1)
                dve.tensor_scalar(r, r, 1.0 / D_MODEL, EPS, ALU.mult, ALU.add).then_inc(tok_mean, 1)
                dve.wait_ge(tok_root, c + 1)
                link(dve.reciprocal(r, r))
                for half in range(2):
                    part = xn[:, c, 512 * half:512 * half + 512]
                    dve.tensor_scalar(part, part, r, None, ALU.mult).then_inc(xn_ready, 1)
                if c == 0:
                    dve.wait_ge(params_landed, 16)
                    dve.tensor_tensor(bias[:, :], col("pool_b", 0, KD), col("pool_scale", 0, KD), ALU.mult
                                      ).then_inc(bias_ready, 1)

            def pooled_residue(m):
                dve.wait_ge(pooled_hi, m + 1)
                dve.scalar_tensor_tensor(out=xlo[:, m, :], in0=bank[m][:, :], scalar=col("g0", m),
                                         in1=xhi_f[:, m, :], op0=ALU.mult, op1=ALU.subtract
                                         ).then_inc(pooled_lo, 1)

            def add_pooled(m):
                dve.wait_ge(wt_used, m // 2 + 1)
                if m < 5:
                    dve.wait_ge(biased, m + 1)
                else:
                    dve.wait_ge(biased_pool, m - 4)
                dve.scalar_tensor_tensor(out=h[:, m, :], in0=bank[m][:, :], scalar=col("pool_scale", m),
                                         in1=h[:, m, :], op0=ALU.mult, op1=ALU.add
                                         ).then_inc(acc_drained if m < 2 else pool_added, 1)

            for m in range(4):
                pooled_residue(m)
            for m in (0, 2):
                pooled_residue(m + 4)
                pooled_residue(m + 5)
                add_pooled(m)
                add_pooled(m + 1)
            for m in (4, 6):
                residue(1, m - 4)
                residue(1, m - 3)
                add_pooled(m)
                add_pooled(m + 1)
            for m in range(4, KD):
                residue(1, m)

            def mlp(u0, a0, hid_base, k, n_next):
                for blk in range(2):
                    with dve.Fori(0, BLK // 2) as i:
                        for e in range(2):
                            dve.wait_ge(wt_used, 2 * (u0 + 32 * blk + e + 1) + 4 * i)
                            count = hid_base + BLK * blk + e
                            a = a0 + 24 * blk + e
                            dve.tensor_scalar(tmp[:, e, :], acc[a % 2][:, :], 0.0, None, ALU.max
                                              ).then_inc(acc_drained, 1)
                            dve.wait_ge(acc_drained, a + 1 + 2 * i)
                            dve.tensor_tensor(tmp[:, e, :], tmp[:, e, :], tmp[:, e, :], ALU.mult
                                              ).then_inc(hid_sq_ready, 1)
                            dve.wait_ge(hid_hi_ready, count + 1 + 2 * i)
                            tile = bass.ds(2 * i + e, 1)
                            dve.tensor_tensor(act_lo[:, tile, :], tmp[:, e:e + 1, :], act_hi_f[:, tile, :],
                                              ALU.subtract).then_inc(hid_lo_ready, 1)
                    if blk == 0:
                        mean(k, rstd, D_MODEL)
                        invert(k, rstd, None)
                        dve.wait_ge(recip_done, k + 1)
                    with dve.Fori(0, KD // 2) as i:
                        for e in range(2):
                            dve.wait_ge(wt_used, 2 * (u0 + 32 * blk + BLK + 2 * e + 2) + 8 * i)
                            a = a0 + 24 * blk + BLK + e
                            tile = bass.ds(2 * i + e, 1)
                            dve.tensor_tensor(tmp[:, e, :], acc[a % 2][:, :], rstd[:, :], ALU.mult
                                              ).then_inc(acc_drained, 1)
                            dve.wait_ge(acc_drained, a + 1 + 2 * i)
                            dve.tensor_tensor(h[:, tile, :], h[:, tile, :], tmp[:, e:e + 1, :], ALU.add
                                              ).then_inc(h_done, 1)
                            if blk == 1 and n_next is not None:
                                residue(n_next, 2 * i + e)

            mlp(U_MLP0, A_MLP0, 0, 0, 2)

            dve.wait_ge(wt_used, 2 * (U_SSM + 1))
            mean(1, rstd, D_MODEL)
            invert(1, rstd, 1)
            dve.wait_ge(recip_done, 2)
            dve.tensor_tensor(tmp[:, 0, :], acc[A_SSM % 2][:, :], rstd[:, :], ALU.mult).then_inc(acc_drained, 1)

            def conv_place(g, q):
                if isinstance(g, int) and g == 0:
                    return U_SSM + 1 + q, 0, q
                return U_GROUP + GT + q, PER_GROUP * (g - 1), CONVS * g + q

            def conv_load(g, q):
                c, r, n = conv_place(g, q)
                a = A_SSM + c - U_SSM
                if c > U_SSM + 1:
                    dve.wait_ge(conv_ready, n)
                dve.wait_ge(wt_used, 2 * (c + 1) + 2 * r)
                dve.tensor_tensor(pre[:, CONV_K - 1:], acc[a % 2][:, :], rstd[:, :], ALU.mult
                                  ).then_inc(acc_drained, 1)

            def conv_tap(g, q, k):
                c, r, n = conv_place(g, q)
                j = c - U_SSM
                out = tmp[:, j % 2, :]
                if k == CONV_K - 1:
                    dve.wait_ge(acc_drained, A_SSM + j + 1 + r)
                    if j >= 3:
                        dve.wait_ge(silu_done, j - 2 + r)
                    if j == 2:
                        dve.wait_ge(dtt_ready, 1)
                    dve.tensor_scalar(out, pre[:, CONV_K - 1:], col("conv_w", 24 * k + n),
                                      col("conv_b", n), ALU.mult, ALU.add).then_inc(conv_step, 1)
                else:
                    dve.wait_ge(conv_step, 3 * n + CONV_K - 1 - k)
                    dve.scalar_tensor_tensor(out=out, in0=pre[:, k:k + TOK], scalar=col("conv_w", 24 * k + n),
                                             in1=out, op0=ALU.mult, op1=ALU.add
                                             ).then_inc(conv_ready if k == 0 else conv_step, 1)

            def conv(g, q):
                conv_load(g, q)
                for k in range(CONV_K - 1, -1, -1):
                    conv_tap(g, q, k)

            dve.wait_ge(consts_landed, 16)
            dve.wait_ge(pads_clear, 1)
            conv(0, 0)
            dve.wait_ge(dtt_ready, 1)
            dt_bias = col("dt_bias", 0, HEADS).unsqueeze(1).to_broadcast(hd4)
            dt_raw = b_misc[:, :].rearrange("p (c n) -> p c n", c=CHUNKS)[:, :, P - HEADS:]
            link(dve.tensor_tensor(dtx[:, :, :], dt_raw, dt_bias, ALU.add))
            dve.scalar_tensor_tensor(out=neg_abs[:, :, :], in0=dtx[:, :, :], scalar=-1.0, in1=dtx[:, :, :],
                                     op0=ALU.mult, op1=ALU.min).then_inc(dt_na, 1)
            link(dve.tensor_scalar(mx[:, :, :], dtx[:, :, :], 0.0, None, ALU.max))
            dve.wait_ge(dt_exp, 2)
            link(dve.tensor_scalar(rc[:, :, :], ex[:, :, :], 2.0, None, ALU.add))
            link(dve.reciprocal(rc[:, :, :], rc[:, :, :]))
            link(dve.tensor_tensor(ex[:, :, :], ex[:, :, :], rc[:, :, :], ALU.mult))
            link(dve.tensor_tensor(s2[:, :, :], ex[:, :, :], ex[:, :, :], ALU.mult))
            link(dve.tensor_scalar(ser[:, :, :], s2[:, :, :], 1.0 / (2 * N_SOFT + 1), None, ALU.mult))
            for n in range(N_SOFT - 1, 0, -1):
                link(dve.scalar_tensor_tensor(out=ser[:, :, :], in0=ser[:, :, :], scalar=1.0 / (2 * n + 1),
                                              in1=s2[:, :, :], op0=ALU.add, op1=ALU.mult))
            link(dve.scalar_tensor_tensor(out=ser[:, :, :], in0=ser[:, :, :], scalar=1.0, in1=ex[:, :, :],
                                          op0=ALU.add, op1=ALU.mult))
            link(dve.scalar_tensor_tensor(out=dt_t[:, :, :], in0=ser[:, :, :], scalar=2.0, in1=mx[:, :, :],
                                          op0=ALU.mult, op1=ALU.add))
            dve.scalar_tensor_tensor(out=adt[:, :, :], in0=dt_t[:, :, :], scalar=-1.0,
                                     in1=exp_a[:, :].unsqueeze(1).to_broadcast(hd4), op0=ALU.mult, op1=ALU.mult
                                     ).then_inc(adt_ready, 1)
            conv(0, 1)
            conv(0, 2)
            dve.wait_ge(cum_ready, 1)
            link(dve.tensor_copy(cum[:, :, :], b_stat[:, 0:2 * P].rearrange("p (a n) -> p a n", a=2)))
            dve.tensor_tensor(dend[:, :], cum[:, 1, :], cum[:, 0, :], ALU.subtract).then_inc(dend_in, 1)
            dve.tensor_copy(acs_f[:, :], bank[2][0:HEADS, :]).then_inc(acsf_ready, 1)
            for q in range(3, CONVS):
                conv(0, q)

            heads3 = [P, HPG, HD]

            def by_head(ap):
                return ap.rearrange("p (h d) -> p h d", h=HPG)

            def of_group(t, c, g, n):
                return t[:, bass.ds(HEADS * c + HPG * g, HPG)].unsqueeze(2).to_broadcast([P, HPG, n])

            def y_chunk(g, c):
                return yx[:, bass.ds(GT * g, GT), P * c:P * c + P]

            def tiles(ap):
                return ap.rearrange("p (i t) -> p i t", i=GT)

            def segment_difference(g, c):
                dve.wait_ge(m_landed[c % 2], 16 * (c // 2 + 1) + 32 * g)
                m = by_head(mbuf[:, c % 2, :])
                dve.tensor_tensor(m, m, of_group(acs_t, c, g, P), ALU.subtract).then_inc(seg_step, 1)

            def segment_limit(g, c):
                dve.wait_ge(seg_step, 4 * g + c + 1)
                dve.tensor_scalar(mbuf[:, c % 2, :], mbuf[:, c % 2, :], 0.0, None, ALU.min).then_inc(seg_ready, 1)

            def decay_times_cb(g, c):
                dve.wait_ge(exp_done, 4 * g + c + 1)
                dve.wait_ge(cbm_ready, g + 1)
                m = by_head(mbuf[:, c % 2, :])
                dve.tensor_tensor(m, m, cbm[:, c:c + 1, :].to_broadcast([P, HPG, P]), ALU.mult
                                  ).then_inc(m_ready, 1)

            def y_diagonal(g, c):
                if c == 0:
                    dve.wait_ge(skip_ready, GT * g + GT)
                dve.wait_ge(yd_ready, 4 * g + c + 1)
                y = y_chunk(g, c)
                dve.tensor_tensor(y, y, tiles(b_yd[:, :]), ALU.add).then_inc(y_step if c else y_done, 1)

            def y_decay(g, c):
                dve.wait_ge(yo_ready, 3 * g + c)
                dve.wait_ge(e_landed[c % 2], 32 * (c // 2 + 1) + 64 * g if c % 2 else 32 + 32 * g)
                dve.tensor_tensor(tiles(ytmp[:, :]), tiles(b_yo[:, :]), e2[:, c % 2, :, :], ALU.mult
                                  ).then_inc(y_step, 1)

            def y_off(g, c):
                dve.wait_ge(y_step, 6 * g + 2 * c)
                y = y_chunk(g, c)
                dve.tensor_tensor(y, y, tiles(ytmp[:, :]), ALU.add).then_inc(y_done, 1)

            def state_decay(g, c):
                dve.wait_ge(state_ready, 3 * g + c)
                dve.tensor_tensor(by_head(state[:, :]), by_head(state[:, :]), of_group(cd, c, g, HD), ALU.mult
                                  ).then_inc(h_step, 1)

            def state_add(g, c):
                dve.wait_ge(st_ready, 3 * g + c + 1)
                if c == 0:
                    dve.tensor_copy(state[:, :], b_st[:, :]).then_inc(state_ready, 1)
                    return
                dve.wait_ge(h_step, 2 * g + c)
                dve.tensor_tensor(state[:, :], state[:, :], b_st[:, :], ALU.add).then_inc(state_ready, 1)

            def token_major(g):
                for c in range(CHUNKS):
                    dve.wait_ge(tok_ready, 6 * g + c + 1)
                    dve.tensor_tensor(by_head(xdt[:, c, :]), by_head(XT_BANK[c][:, :]),
                                      of_group(dt_t[:, :, :].rearrange("p c h -> p (c h)"), c, g, HD), ALU.mult
                                      ).then_inc(xdt_ready, 1)
                dve.wait_ge(tok_ready, 6 * g + 6)
                dve.tensor_tensor(cbm[:, :, :], b_stat[:, :].rearrange("p (c t) -> p c t", c=CHUNKS),
                                  upper.unsqueeze(1).to_broadcast([P, CHUNKS, P]), ALU.mult).then_inc(cbm_ready, 1)

            def gate(g):
                dve.wait_ge(y_done, 4 * g + 4)
                y = yx[:, bass.ds(GT * g, GT), :]
                dve.tensor_tensor(y, y, zs[:, bass.ds(GT * g, GT), :], ALU.mult).then_inc(gated, 1)

            def take_spread(g):
                dve.wait_ge(spread_ready, g + 1)
                dve.tensor_scalar(rg[:, :], b_stat[:, :], 1.0, None, ALU.mult).then_inc(recip_done, 1)

            def norm_y(g, i):
                dve.wait_ge(recip_done, SSM_STAT + g + 1)
                y = yx[:, bass.ds(GT * g + i, 1), :]
                dve.scalar_tensor_tensor(out=y, in0=y, scalar=col("norm_g", GT * g + i),
                                         in1=rg[:, :].unsqueeze(1), op0=ALU.mult, op1=ALU.mult
                                         ).then_inc(yn_ready, 1)

            def norm_hi(g, i):
                dve.wait_ge(yn_ready, GT * g + i + 1)
                tile = bass.ds(GT * g + i, 1)
                dve.tensor_scalar(act_hi[:, tile, :], yx[:, tile, :], 1.0, None, ALU.mult).then_inc(yhi_ready, 1)

            def zgate(g, r, t):
                a = A_SSM + 7 + t
                dve.wait_ge(wt_used, 2 * (U_GROUP + t + 1) + 2 * r)
                dve.wait_ge(silu_done, 7 + t - 2 + r)
                dve.tensor_tensor(tmp[:, (7 + t) % 2, :], acc[a % 2][:, :], rstd[:, :], ALU.mult
                                  ).then_inc(acc_drained, 1)

            def add_chunk(g, c):
                y_diagonal(g, c)
                if c:
                    y_decay(g, c)
                if 0 < c < CHUNKS - 1:
                    state_decay(g, c)
                if c:
                    y_off(g, c)
                if c < CHUNKS - 1:
                    state_add(g, c)

            def group(g, r, first=False, last=False):
                sched = CHUNK_AFTER_LAST if last else CHUNK_AFTER
                segs = SEGMENT_AT_LAST if last else SEGMENT_AT
                for t in range(PER_GROUP + (2 if last else 0)):
                    c_next = sched.get(t + 1)
                    if c_next is not None and t not in segs:
                        decay_times_cb(g, c_next)
                    if t < GT or last:
                        if t in segs:
                            segment_difference(g, segs[t])
                        if t < GT:
                            zgate(g, r, t)
                        if t in segs:
                            segment_limit(g, segs[t])
                        if t >= GT:
                            add_output(t - GT)
                        if t == 0:
                            token_major(g)
                        if not first and t == T_GATE:
                            gate(g - 1)
                        if last and not first and t == T_STAT:
                            diagonals(SSM_STAT - 1 + g, D_INNER // GROUPS, 1 + g)
                        if t in sched:
                            add_chunk(g, sched[t])
                        if c_next is not None and t in segs:
                            decay_times_cb(g, c_next)
                        if last and t == T_STAT + 1:
                            take_spread(g - 1)
                        if last and t == 6:
                            gate(g)
                        if last and t in T_NORM_LAST:
                            i = 0 if t == T_NORM_LAST[0] else 2
                            norm_y(g - 1, i)
                            norm_y(g - 1, i + 1)
                            norm_hi(g - 1, i)
                            norm_hi(g - 1, i + 1)
                        if last and t == 9:
                            diagonals(SSM_STAT + g, D_INNER // GROUPS, 2 + g)
                            take_spread(g)
                            for i in range(GT + 1):
                                if i < GT:
                                    norm_y(g, i)
                                if i:
                                    norm_hi(g, i - 1)
                        continue
                    q, c = t - GT, sched.get(t - 1)
                    i = None if first else {T_NORM[0]: 0, T_NORM[1]: 2}.get(t)
                    if not first and t == T_STAT + 1:
                        take_spread(g - 1)
                    if t in segs:
                        segment_difference(g, segs[t])
                    conv_load(g + 1, q)
                    if t in segs:
                        segment_limit(g, segs[t])
                    if c is not None:
                        y_diagonal(g, c)
                    conv_tap(g + 1, q, 3)
                    if c is not None:
                        y_decay(g, c)
                    if i is not None:
                        norm_y(g - 1, i)
                    conv_tap(g + 1, q, 2)
                    if c is not None:
                        if c < CHUNKS - 1:
                            state_decay(g, c)
                            y_off(g, c)
                    if i is not None:
                        norm_hi(g - 1, i)
                        norm_y(g - 1, i + 1)
                    conv_tap(g + 1, q, 1)
                    if c is not None and c < CHUNKS - 1:
                        state_add(g, c)
                    if i is not None:
                        norm_hi(g - 1, i + 1)
                    conv_tap(g + 1, q, 0)
                    if c == CHUNKS - 1:
                        y_off(g, c)
                    if c_next is not None and t in segs:
                        decay_times_cb(g, c_next)
                    if not first and t == T_STAT:
                        diagonals(SSM_STAT - 1 + g, D_INNER // GROUPS, 1 + g)

            def add_output(n):
                a, m = A_OUT + n, n % KD
                dve.wait_ge(wt_used, 2 * (U_OUT + n + 1))
                dve.tensor_tensor(h[:, m, :], h[:, m, :], acc[a % 2][:, :], ALU.add).then_inc(acc_drained, 1)

            group(0, 0, first=True)
            with dve.Fori(1, GROUPS - 1) as g:
                group(g, PER_GROUP * g)
            group(GROUPS - 1, PER_GROUP * (GROUPS - 1), last=True)
            for m in range(KD):
                add_output(KD + m)
                residue(3, m)

            mlp(U_MLP1, A_MLP1, 32, 6, None)
            dve.wait_ge(stat_ready, 8)
            for c in range(CHUNKS):
                last = dve.tensor_scalar(r_tok[:, c:c + 1], bank[2 + c][:, 0:1], 1.0 / D_MODEL, EPS,
                                         ALU.mult, ALU.add)
            last.then_inc(stat_drained, 1)
            make_diagonals(6)
            dve.wait_ge(spread_ready, GROUPS + 1)
            for m in range(KD):
                dve.wait_ge(hg_ready, m + 1)
                dve.tensor_tensor(hg[:, m, :], hg[:, m, :], b_stat[:, :], ALU.mult).then_inc(out_ready, 1)


def kernel(**inputs):
    import numpy as np
    import concourse.bacc as bacc
    from concourse.bass_utils import run_bass_kernel_spmd

    a = {k: np.asarray(v) for k, v in inputs.items()}

    def units(w, k_tiles=8):
        k, n = w.shape
        t = w.reshape(k // (P * k_tiles), k_tiles, P, n // P, P)
        return t.transpose(3, 0, 2, 1, 4).reshape(-1, P, k_tiles * P)

    def mlp(i):
        w1, w2 = a["mlp_w1"][i], a["mlp_w2"][i]
        parts = []
        for blk in range(2):
            cols = slice(blk * BLK * P, (blk + 1) * BLK * P)
            parts += [units(w1[:, cols]), units(w2[cols, :])]
        return parts

    pw = a["pool_w"][0].reshape(2, 2, 2, P, 2, P)
    pool = pw.transpose(0, 3, 1, 4, 2, 5).reshape(2, P, 8 * P)
    w_in = a["ssm_w_in"][0]
    z0, x0, b0, c0 = 0, D_INNER, 2 * D_INNER, 2 * D_INNER + GROUPS * P
    gw = GT * P

    def conv_cols(g):
        return np.r_[b0 - x0 + g * P:b0 - x0 + (g + 1) * P, c0 - x0 + g * P:c0 - x0 + (g + 1) * P,
                     g * gw:(g + 1) * gw]

    ssm = [units(w_in[:, -P:]), units(w_in[:, x0 + conv_cols(0)])]
    for g in range(GROUPS):
        ssm.append(units(w_in[:, z0 + g * gw:z0 + (g + 1) * gw]))
        if g + 1 < GROUPS:
            ssm.append(units(w_in[:, x0 + conv_cols(g + 1)]))
    w_out = a["ssm_w_out"][0]
    out = [units(w_out[:1024]), units(w_out[1024:])]
    weights = np.concatenate([pool, *mlp(0), *ssm, *out, *mlp(1)])
    assert weights.shape[0] == UNITS

    def tiles(v):
        return v.reshape(-1, P).T

    channels = np.concatenate([conv_cols(g) for g in range(GROUPS)])
    rows = lambda v: np.broadcast_to(v, (P, v.shape[-1]))
    table = {
        "g0": tiles(a["norm_mix_g"][0]), "g1": tiles(a["norm_mlp_g"][0]),
        "g2": tiles(a["norm_mix_g"][1]), "g3": tiles(a["norm_mlp_g"][1]), "gf": tiles(a["final_g"]),
        "pool_b": tiles(a["pool_b"][0]), "pool_scale": tiles(a["pool_scale"][0]),
        "conv_w": np.concatenate([tiles(a["ssm_conv_w"][0][k][channels]) for k in range(CONV_K)], axis=1),
        "conv_b": tiles(a["ssm_conv_b"][0][channels]), "norm_g": tiles(a["ssm_norm_g"][0]),
        "skip": tiles(np.repeat(a["ssm_d"][0], HD)),
        "dt_bias": rows(a["ssm_dt_bias"][0]), "a_log": rows(a["ssm_a_log"][0]),
    }
    params = np.concatenate([table[k] for k in COLS], axis=1)
    consts = np.concatenate([np.ones((P, P)), np.triu(np.ones((P, P))), np.eye(P)], axis=1)
    s, l = np.arange(P)[:, None], np.arange(P)[None, :]
    mats = []
    for w in WINDOWS:
        near = (l >= s) & (l - s < w)
        first = near / np.minimum(l + 1, w) - (l == s)
        later = near / w - (l == s)
        before = ((l + P - s < w) / w)[:, :REACH]
        mats.append(np.concatenate([first, before, later, before], axis=1))
    pooling = np.stack(mats, axis=1)
    arrays = {"xt": a["x"][0].T.reshape(KD, P, TOK), "x_tok": a["x"][0].reshape(CHUNKS, P, D_MODEL),
              "pooling": pooling.astype(np.float32), "weights": weights, "params": params,
              "consts": consts.astype(np.float32)}
    arrays = {k: np.ascontiguousarray(v) for k, v in arrays.items()}

    nc = bacc.Bacc("TRN2", target_bir_lowering=False, num_devices=1)
    args = [nc.dram_tensor(k, list(v.shape), F32, kind="ExternalInput").ap() for k, v in arrays.items()]
    out_t = nc.dram_tensor("out_t", [KD, P, TOK], F32, kind="ExternalOutput").ap()
    build(nc, *args, out_t)
    r = run_bass_kernel_spmd(nc, [arrays], core_ids=[0])
    return np.ascontiguousarray(r.results[0]["out_t"].reshape(D_MODEL, TOK).T)[None]
```
